# Optimizing a Trainium2 kernel written in Bass

```python
import math
import jax, jax.numpy as jnp
from jax import lax
import numpy as np

D_MODEL = 1024
BATCH = 1
SEQ = 512
DEPTH = 2

N_MEM = 256
EPS = 1e-6
SEQ_WIDTH = 2 * D_MODEL
XA_HEADS = 4
XA_HEAD_DIM = D_MODEL // XA_HEADS
XA_WIDTH = XA_HEADS * XA_HEAD_DIM
MIX_WIDTH = SEQ_WIDTH + XA_WIDTH
GLA_HEADS = 4
GLA_DK = (D_MODEL // 2) // GLA_HEADS
GLA_DV = SEQ_WIDTH // GLA_HEADS
GLA_RANK = 16
GLA_TAU = 16.0
GLA_CHUNK = 64
S5_GROUP = 16
S5_GROUPS = SEQ_WIDTH // S5_GROUP
S5_STATE = 64
S5_CHUNK = 128
S5_DT_MIN = 1e-3
S5_DT_MAX = 1e-1
GLA_IN = 2 * GLA_HEADS * GLA_DK + SEQ_WIDTH + GLA_RANK + MIX_WIDTH + XA_WIDTH
S5_IN = SEQ_WIDTH + MIX_WIDTH + XA_WIDTH
N_GLA = (DEPTH + 1) // 2
N_S5 = DEPTH // 2


def rms_norm(x, w):
    xf = x.astype(jnp.float32)
    y = xf * lax.rsqrt(jnp.mean(xf * xf, axis=-1, keepdims=True) + EPS)
    return (y * w.astype(jnp.float32)).astype(x.dtype)

def split_cols(t, sizes):
    idx = np.cumsum(sizes)[:-1].tolist()
    return jnp.split(t, idx, axis=-1)

def memory_attention(q, mem_n, w_kv):
    b_, l_, _ = q.shape
    k, v = jnp.split(mem_n @ w_kv, 2, axis=-1)
    qh = q.reshape(b_, l_, XA_HEADS, XA_HEAD_DIM)
    kh = k.reshape(b_, -1, XA_HEADS, XA_HEAD_DIM)
    vh = v.reshape(b_, -1, XA_HEADS, XA_HEAD_DIM)
    s = jnp.einsum('blhd,bmhd->bhlm', qh, kh).astype(jnp.float32) * (XA_HEAD_DIM ** -0.5)
    p = jax.nn.softmax(s, axis=-1).astype(v.dtype)
    o = jnp.einsum('bhlm,bmhd->blhd', p, vh)
    return o.reshape(b_, l_, XA_WIDTH)

def gla_chunked(q, k, v, g):
    b_, l_, h_, dk = q.shape
    dv = v.shape[-1]
    nc = l_ // GLA_CHUNK

    def to_chunks(t):
        return t.reshape(b_, nc, GLA_CHUNK, h_, t.shape[-1]).transpose(1, 0, 3, 2, 4)

    qc, kc, vc, gc = to_chunks(q), to_chunks(k), to_chunks(v), to_chunks(g)
    causal = jnp.tril(jnp.ones((GLA_CHUNK, GLA_CHUNK), dtype=bool))

    def step(state, inp):
        qi, ki, vi, gi = inp
        qf, kf, vf = qi.astype(jnp.float32), ki.astype(jnp.float32), vi.astype(jnp.float32)
        bcum = jnp.cumsum(gi.astype(jnp.float32), axis=-2)
        b_last = bcum[..., -1:, :]
        q_dec = qf * jnp.exp(bcum)
        k_inv = kf * jnp.exp(-bcum)
        k_end = kf * jnp.exp(b_last - bcum)
        att = jnp.where(causal, jnp.einsum('bhcd,bhsd->bhcs', q_dec, k_inv), 0.0)
        o = jnp.einsum('bhcs,bhse->bhce', att, vf) + jnp.einsum('bhcd,bhde->bhce', q_dec, state)
        state = jnp.exp(b_last[..., 0, :])[..., None] * state + jnp.einsum('bhcd,bhce->bhde', k_end, vf)
        return state, o.astype(v.dtype)

    s0 = jnp.zeros((b_, h_, dk, dv), jnp.float32)
    _, o = lax.scan(step, s0, (qc, kc, vc, gc))
    return o.transpose(1, 0, 3, 2, 4).reshape(b_, l_, h_, dv)

def gla_branch(h, w_in, w_gate_up, gate_bias, out_norm_w):
    b_, l_, _ = h.shape
    qk = GLA_HEADS * GLA_DK
    q, k, v, r, z, xq = split_cols(h @ w_in, [qk, qk, SEQ_WIDTH, GLA_RANK, MIX_WIDTH, XA_WIDTH])
    g = jax.nn.log_sigmoid((r @ w_gate_up + gate_bias).astype(jnp.float32)) / GLA_TAU
    o = gla_chunked(q.reshape(b_, l_, GLA_HEADS, GLA_DK) * (GLA_DK ** -0.5),
                    k.reshape(b_, l_, GLA_HEADS, GLA_DK),
                    v.reshape(b_, l_, GLA_HEADS, GLA_DV),
                    g.reshape(b_, l_, GLA_HEADS, GLA_DK))
    o = rms_norm(o, out_norm_w).reshape(b_, l_, SEQ_WIDTH)
    return o.astype(h.dtype), z, xq

def s5_discretize(lam_re, lam_im, log_step, b_re, b_im):
    lam_re = lam_re.astype(jnp.float32)
    lam_im = lam_im.astype(jnp.float32)
    dt = jnp.exp(log_step.astype(jnp.float32))[:, None]
    mag = jnp.exp(lam_re * dt)
    ab_re = mag * jnp.cos(lam_im * dt)
    ab_im = mag * jnp.sin(lam_im * dt)
    den = lam_re * lam_re + lam_im * lam_im
    nr, ni = ab_re - 1.0, ab_im
    coef_re = ((nr * lam_re + ni * lam_im) / den)[..., None]
    coef_im = ((ni * lam_re - nr * lam_im) / den)[..., None]
    br, bi = b_re.astype(jnp.float32), b_im.astype(jnp.float32)
    bb_re = coef_re * br - coef_im * bi
    bb_im = coef_re * bi + coef_im * br
    return ab_re, ab_im, bb_re, bb_im

def _linrec_combine(e1, e2):
    a1r, a1i, x1r, x1i = e1
    a2r, a2i, x2r, x2i = e2
    return (a1r * a2r - a1i * a2i,
            a1r * a2i + a1i * a2r,
            a2r * x1r - a2i * x1i + x2r,
            a2r * x1i + a2i * x1r + x2i)

def s5_chunked(u, ab_re, ab_im, bb_re, bb_im, c_re, c_im):
    b_, l_, g_, hg = u.shape
    nc = l_ // S5_CHUNK
    uc = u.reshape(b_, nc, S5_CHUNK, g_, hg).transpose(1, 0, 2, 3, 4)

    def step(carry, u_i):
        cr, ci = carry
        bu_re = jnp.einsum('bcgh,gph->bcgp', u_i, bb_re)
        bu_im = jnp.einsum('bcgh,gph->bcgp', u_i, bb_im)
        a_r = jnp.broadcast_to(ab_re, bu_re.shape)
        a_i = jnp.broadcast_to(ab_im, bu_im.shape)
        acum_r, acum_i, x_r, x_i = lax.associative_scan(_linrec_combine, (a_r, a_i, bu_re, bu_im), axis=1)
        x_r = x_r + acum_r * cr[:, None] - acum_i * ci[:, None]
        x_i = x_i + acum_r * ci[:, None] + acum_i * cr[:, None]
        y = jnp.einsum('bcgp,ghp->bcgh', x_r, c_re) - jnp.einsum('bcgp,ghp->bcgh', x_i, c_im)
        return (x_r[:, -1], x_i[:, -1]), y

    zeros = jnp.zeros((b_, g_, S5_STATE), jnp.float32)
    _, y = lax.scan(step, (zeros, zeros), uc)
    return y.transpose(1, 0, 2, 3, 4).reshape(b_, l_, g_, hg)

def s5_branch(h, w_in, lam_re, lam_im, log_step, b_re, b_im, c_re, c_im, d, w_glu, b_glu):
    b_, l_, _ = h.shape
    u, z, xq = split_cols(h @ w_in, [SEQ_WIDTH, MIX_WIDTH, XA_WIDTH])
    ab_re, ab_im, bb_re, bb_im = s5_discretize(lam_re, lam_im, log_step, b_re, b_im)
    uf = u.astype(jnp.float32)
    y = s5_chunked(uf.reshape(b_, l_, S5_GROUPS, S5_GROUP), ab_re, ab_im, bb_re, bb_im,
                   c_re.astype(jnp.float32), c_im.astype(jnp.float32))
    y = y.reshape(b_, l_, SEQ_WIDTH) + d.astype(jnp.float32) * uf
    y = jax.nn.gelu(y).astype(h.dtype)
    y = y * jax.nn.sigmoid(y @ w_glu + b_glu)
    return y, z, xq

def first_inputs(seed: int = 0) -> dict:
    key = jax.random.key(seed)
    ks = jax.random.split(key, 24)
    nrm = jax.random.normal
    inv = lambda n: 1.0 / math.sqrt(n)
    n_idx = jnp.arange(S5_STATE, dtype=jnp.float32)
    lam_re = -0.5 * jnp.exp(0.02 * nrm(ks[8], (N_S5, S5_GROUPS, S5_STATE), jnp.float32))
    lam_im = jnp.broadcast_to(math.pi * n_idx, (N_S5, S5_GROUPS, S5_STATE)).astype(jnp.float32)
    log_step = jax.random.uniform(ks[9], (N_S5, S5_GROUPS), jnp.float32,
                                  math.log(S5_DT_MIN), math.log(S5_DT_MAX))
    return {
        "x": nrm(ks[0], (BATCH, SEQ, D_MODEL), jnp.float32),
        "mem": nrm(ks[1], (BATCH, N_MEM, D_MODEL), jnp.float32),
        "norm_w": 1.0 + 0.02 * nrm(ks[2], (DEPTH, D_MODEL), jnp.float32),
        "mem_norm_w": 1.0 + 0.02 * nrm(ks[3], (D_MODEL,), jnp.float32),
        "gla_w_in": nrm(ks[4], (N_GLA, D_MODEL, GLA_IN), jnp.float32) * inv(D_MODEL),
        "gla_w_gate_up": nrm(ks[5], (N_GLA, GLA_RANK, GLA_HEADS * GLA_DK), jnp.float32) * inv(GLA_RANK),
        "gla_gate_bias": 0.1 * nrm(ks[6], (N_GLA, GLA_HEADS * GLA_DK), jnp.float32),
        "gla_out_norm_w": 1.0 + 0.02 * nrm(ks[7], (N_GLA, GLA_DV), jnp.float32),
        "s5_w_in": nrm(ks[10], (N_S5, D_MODEL, S5_IN), jnp.float32) * inv(D_MODEL),
        "s5_lam_re": lam_re,
        "s5_lam_im": lam_im,
        "s5_log_step": log_step,
        "s5_b_re": nrm(ks[11], (N_S5, S5_GROUPS, S5_STATE, S5_GROUP), jnp.float32) * inv(2 * S5_GROUP),
        "s5_b_im": nrm(ks[12], (N_S5, S5_GROUPS, S5_STATE, S5_GROUP), jnp.float32) * inv(2 * S5_GROUP),
        "s5_c_re": 0.5 * nrm(ks[13], (N_S5, S5_GROUPS, S5_GROUP, S5_STATE), jnp.float32),
        "s5_c_im": 0.5 * nrm(ks[14], (N_S5, S5_GROUPS, S5_GROUP, S5_STATE), jnp.float32),
        "s5_d": nrm(ks[15], (N_S5, SEQ_WIDTH), jnp.float32),
        "s5_w_glu": nrm(ks[16], (N_S5, SEQ_WIDTH, SEQ_WIDTH), jnp.float32) * inv(SEQ_WIDTH),
        "s5_b_glu": 0.01 * nrm(ks[17], (N_S5, SEQ_WIDTH), jnp.float32),
        "xa_w_kv": nrm(ks[18], (DEPTH, D_MODEL, 2 * XA_WIDTH), jnp.float32) * inv(D_MODEL),
        "w_out": nrm(ks[19], (DEPTH, MIX_WIDTH, D_MODEL), jnp.float32) * inv(MIX_WIDTH),
        "final_norm_w": 1.0 + 0.02 * nrm(ks[20], (D_MODEL,), jnp.float32),
    }

def first_block(x, mem, norm_w, mem_norm_w, gla_w_in, gla_w_gate_up, gla_gate_bias, gla_out_norm_w,
              s5_w_in, s5_lam_re, s5_lam_im, s5_log_step, s5_b_re, s5_b_im, s5_c_re, s5_c_im,
              s5_d, s5_w_glu, s5_b_glu, xa_w_kv, w_out, final_norm_w):
    mem_n = rms_norm(mem, mem_norm_w)
    for i in range(DEPTH):
        h = rms_norm(x, norm_w[i])
        j = i // 2
        if i % 2 == 0:
            seq_out, z, xq = gla_branch(h, gla_w_in[j], gla_w_gate_up[j], gla_gate_bias[j], gla_out_norm_w[j])
        else:
            seq_out, z, xq = s5_branch(h, s5_w_in[j], s5_lam_re[j], s5_lam_im[j], s5_log_step[j],
                                       s5_b_re[j], s5_b_im[j], s5_c_re[j], s5_c_im[j],
                                       s5_d[j], s5_w_glu[j], s5_b_glu[j])
        xa = memory_attention(xq, mem_n, xa_w_kv[i])
        y = jnp.concatenate([seq_out.astype(x.dtype), xa.astype(x.dtype)], axis=-1) * jax.nn.silu(z)
        x = x + y @ w_out[i]
    return rms_norm(x, final_norm_w)


N_META = 16
RMS_EPS = 1e-6
D_FF = 4 * D_MODEL
N_EVEN = (DEPTH + 1) // 2
N_ODD = DEPTH // 2
RWKV_HEAD = 64
RWKV_WIDTH = D_MODEL // 2
RWKV_HEADS = RWKV_WIDTH // RWKV_HEAD
DECAY_RANK = 64
ICLR_RANK = 64
GATE_RANK = 128
GN_EPS = RWKV_HEAD * 1e-5
POOL_WIDTH = D_MODEL - RWKV_WIDTH
POOL_WINDOWS = (2, 4, 8, 16)
POOL_GROUPS = len(POOL_WINDOWS)
POOL_GROUP_W = POOL_WIDTH // POOL_GROUPS
SHIFT_WIDTH = 3 * RWKV_WIDTH + DECAY_RANK + ICLR_RANK + GATE_RANK
EVEN_IN = SHIFT_WIDTH + POOL_WIDTH
RWKV_SPLITS = (RWKV_WIDTH, 2 * RWKV_WIDTH, 3 * RWKV_WIDTH,
               3 * RWKV_WIDTH + DECAY_RANK, 3 * RWKV_WIDTH + DECAY_RANK + ICLR_RANK)
DIFF_HEADS = 8
DIFF_HEAD = D_MODEL // (2 * DIFF_HEADS)
DIFF_IN = 3 * D_MODEL
SUBLN_EPS = 1e-5
ROPE_THETA = 10000.0
Q_BLOCK = 128


def rmsnorm(t, g, eps=RMS_EPS):
    tf = t.astype(jnp.float32)
    tf = tf * lax.rsqrt(jnp.mean(tf * tf, axis=-1, keepdims=True) + eps)
    return (tf * g.astype(jnp.float32)).astype(t.dtype)

def rope_tables(length):
    pos = jnp.arange(length, dtype=jnp.float32)
    inv = ROPE_THETA ** (-jnp.arange(0, DIFF_HEAD, 2, dtype=jnp.float32) / DIFF_HEAD)
    ang = pos[:, None] * inv[None, :]
    ang = jnp.concatenate([ang, ang], axis=-1)
    return jnp.cos(ang), jnp.sin(ang)

def apply_rope(t, cos, sin):
    tf = t.astype(jnp.float32)
    t1, t2 = jnp.split(tf, 2, axis=-1)
    rot = jnp.concatenate([-t2, t1], axis=-1)
    c = cos[None, :, None, None, :]
    s = sin[None, :, None, None, :]
    return (tf * c + rot * s).astype(t.dtype)

def rwkv7_scan(r, decay, k, v, kk, a):
    B, L, H, N = r.shape

    def step(S, inp):
        r_t, w_t, k_t, v_t, kk_t, a_t = inp
        sa = jnp.einsum('bhvk,bhk->bhv', S, -kk_t)
        S = (S * w_t[:, :, None, :]
             + sa[..., None] * (kk_t * a_t)[:, :, None, :]
             + v_t[..., None] * k_t[:, :, None, :])
        o = jnp.einsum('bhvk,bhk->bhv', S, r_t)
        return S, o

    xs = tuple(jnp.moveaxis(t, 1, 0) for t in (r, decay, k, v, kk, a))
    S0 = jnp.zeros((B, H, N, N), jnp.float32)
    _, o = lax.scan(step, S0, xs)
    return jnp.moveaxis(o, 0, 1)

def rwkv_pool_mixer(h, w_in, mu, w0, w_up, a0, a_up, g_up, k_k, k_a, r_k,
                    ln_w, ln_b, pool_w, pool_scale, w_out):
    B, L, _ = h.shape
    f32 = jnp.float32
    y = h @ w_in
    ys = y[..., :SHIFT_WIDTH]
    prev = jnp.pad(ys, ((0, 0), (1, 0), (0, 0)))[:, :L]
    ys = ys + (prev - ys) * mu
    r, k, v, wd, ad, gd = jnp.split(ys, RWKV_SPLITS, axis=-1)
    wlog = -jax.nn.softplus(-(w0 + jnp.tanh(wd) @ w_up).astype(f32)) - 0.5
    decay = jnp.exp(-jnp.exp(wlog))
    a = jax.nn.sigmoid((a0 + ad @ a_up).astype(f32))
    g = (jax.nn.sigmoid(gd) @ g_up).astype(f32)
    hs = lambda t: t.reshape(B, L, RWKV_HEADS, RWKV_HEAD)
    kf = k.astype(f32)
    kk = hs(kf * k_k)
    kk = kk / jnp.maximum(jnp.linalg.norm(kk, axis=-1, keepdims=True), 1e-12)
    kf = kf * (1.0 + (a - 1.0) * k_a)
    rf, kf, vf, a_h, dec = hs(r.astype(f32)), hs(kf), hs(v.astype(f32)), hs(a), hs(decay)
    o = rwkv7_scan(rf, dec, kf, vf, kk, a_h)
    mean = jnp.mean(o, axis=-1, keepdims=True)
    var = jnp.mean(jnp.square(o - mean), axis=-1, keepdims=True)
    o = ((o - mean) * lax.rsqrt(var + GN_EPS)).reshape(B, L, RWKV_WIDTH) * ln_w + ln_b
    bonus = jnp.sum(rf * kf * r_k, axis=-1, keepdims=True) * vf
    o = ((o + bonus.reshape(B, L, RWKV_WIDTH)) * g).astype(h.dtype)
    u = y[..., SHIFT_WIDTH:].reshape(B, L, POOL_GROUPS, POOL_GROUP_W).astype(f32)
    t_idx = jnp.arange(L)
    diffs = []
    for gi, win in enumerate(POOL_WINDOWS):
        ug = u[:, :, gi]
        c = jnp.cumsum(ug, axis=1)
        lag = jnp.pad(c, ((0, 0), (win, 0), (0, 0)))[:, :L]
        cnt = jnp.minimum(t_idx + 1, win).astype(f32)[None, :, None]
        diffs.append((c - lag) / cnt - ug)
    d = jnp.stack(diffs, axis=2)
    z = jnp.einsum('blgc,gcd->blgd', d, pool_w.astype(f32)).reshape(B, L, POOL_WIDTH)
    z = (z * pool_scale).astype(h.dtype)
    return jnp.concatenate([o, z], axis=-1) @ w_out

def causal_diff_attention(q, k, v, lam):
    B, L, H, _, dh = q.shape
    nb = -(-L // Q_BLOCK)
    Lp = nb * Q_BLOCK
    pad = Lp - L
    q = jnp.pad(q, ((0, 0), (0, pad), (0, 0), (0, 0), (0, 0)))
    k = jnp.pad(k, ((0, 0), (0, pad), (0, 0), (0, 0), (0, 0)))
    v = jnp.pad(v, ((0, 0), (0, pad), (0, 0), (0, 0)))
    qb = jnp.moveaxis(q.reshape(B, nb, Q_BLOCK, H, 2, dh), 1, 0)
    kpos = jnp.arange(Lp)
    scale = DIFF_HEAD ** -0.5

    def one_block(args):
        qblk, start = args
        s = jnp.einsum('bqhcd,bkhcd->bhcqk', qblk, k).astype(jnp.float32) * scale
        qpos = start + jnp.arange(Q_BLOCK)
        mask = kpos[None, :] <= qpos[:, None]
        s = jnp.where(mask, s, -jnp.inf)
        p = jax.nn.softmax(s, axis=-1)
        attn = p[:, :, 0] - lam * p[:, :, 1]
        return jnp.einsum('bhqk,bkhe->bqhe', attn.astype(v.dtype), v)

    out = lax.map(one_block, (qb, jnp.arange(nb) * Q_BLOCK))
    out = jnp.moveaxis(out, 0, 1).reshape(B, Lp, H, 2 * dh)
    return out[:, :L]

def diff_attn_mixer(h, w_in, lam_vecs, subln_w, w_out, cos, sin, layer):
    B, L, _ = h.shape
    y = h @ w_in
    q, k, v = jnp.split(y, 3, axis=-1)
    q = apply_rope(q.reshape(B, L, DIFF_HEADS, 2, DIFF_HEAD), cos, sin)
    k = apply_rope(k.reshape(B, L, DIFF_HEADS, 2, DIFF_HEAD), cos, sin)
    v = v.reshape(B, L, DIFF_HEADS, 2 * DIFF_HEAD)
    lam_init = 0.8 - 0.6 * math.exp(-0.3 * layer)
    lv = lam_vecs.astype(jnp.float32)
    lam = jnp.exp(jnp.sum(lv[0] * lv[1])) - jnp.exp(jnp.sum(lv[2] * lv[3])) + lam_init
    o = causal_diff_attention(q, k, v, lam)
    o = rmsnorm(o, subln_w, SUBLN_EPS) * (1.0 - lam_init)
    return o.reshape(B, L, D_MODEL).astype(h.dtype) @ w_out

def sq_relu_mlp(h, w1, w2):
    return jnp.square(jax.nn.relu(h @ w1)) @ w2

def second_inputs(seed: int = 0) -> dict:
    key = jax.random.key(seed)
    ks = jax.random.split(key, 24)
    nrm = lambda i, shape, s: jax.random.normal(ks[i], shape, jnp.float32) * s
    RW = RWKV_WIDTH
    return {
        'x': nrm(0, (BATCH, SEQ, D_MODEL), 1.0),
        'meta': nrm(1, (N_META, D_MODEL), 1.0),
        'norm_g': 1.0 + nrm(2, (DEPTH, 4, D_MODEL), 0.1),
        'mlp_w1': nrm(3, (DEPTH, D_MODEL, D_FF), D_MODEL ** -0.5),
        'mlp_w2': nrm(4, (DEPTH, D_FF, D_MODEL), D_FF ** -0.5),
        'ev_w_in': nrm(5, (N_EVEN, D_MODEL, EVEN_IN), D_MODEL ** -0.5),
        'ev_mu': jax.random.uniform(ks[6], (N_EVEN, SHIFT_WIDTH), jnp.float32),
        'ev_w0': jax.random.uniform(ks[7], (N_EVEN, RW), jnp.float32, -4.0, 1.0),
        'ev_w_up': nrm(8, (N_EVEN, DECAY_RANK, RW), 0.5 * DECAY_RANK ** -0.5),
        'ev_a0': nrm(9, (N_EVEN, RW), 0.1),
        'ev_a_up': nrm(10, (N_EVEN, ICLR_RANK, RW), ICLR_RANK ** -0.5),
        'ev_g_up': nrm(11, (N_EVEN, GATE_RANK, RW), GATE_RANK ** -0.5),
        'ev_k_k': 0.85 + nrm(12, (N_EVEN, RW), 0.05),
        'ev_k_a': 1.0 + nrm(13, (N_EVEN, RW), 0.05),
        'ev_r_k': nrm(14, (N_EVEN, RWKV_HEADS, RWKV_HEAD), 0.1),
        'ev_ln_w': 1.0 + nrm(15, (N_EVEN, RW), 0.1),
        'ev_ln_b': nrm(16, (N_EVEN, RW), 0.02),
        'ev_pool_w': nrm(17, (N_EVEN, POOL_GROUPS, POOL_GROUP_W, POOL_GROUP_W), POOL_GROUP_W ** -0.5),
        'ev_pool_scale': 1.0 + nrm(18, (N_EVEN, POOL_WIDTH), 0.1),
        'ev_w_out': nrm(19, (N_EVEN, D_MODEL, D_MODEL), D_MODEL ** -0.5),
        'od_w_in': nrm(20, (N_ODD, D_MODEL, DIFF_IN), D_MODEL ** -0.5),
        'od_lambda': nrm(21, (N_ODD, 4, DIFF_HEAD), 0.1),
        'od_subln_w': 1.0 + nrm(22, (N_ODD, 2 * DIFF_HEAD), 0.1),
        'od_w_out': nrm(23, (N_ODD, D_MODEL, D_MODEL), D_MODEL ** -0.5),
    }

def second_block(x, meta, norm_g, mlp_w1, mlp_w2, ev_w_in, ev_mu, ev_w0, ev_w_up, ev_a0,
              ev_a_up, ev_g_up, ev_k_k, ev_k_a, ev_r_k, ev_ln_w, ev_ln_b, ev_pool_w,
              ev_pool_scale, ev_w_out, od_w_in, od_lambda, od_subln_w, od_w_out):
    B = x.shape[0]
    h = jnp.concatenate([jnp.broadcast_to(meta[None].astype(x.dtype), (B, N_META, D_MODEL)), x], axis=1)
    L = h.shape[1]
    cos, sin = rope_tables(L)
    for i in range(DEPTH):
        g = norm_g[i]
        j = i // 2
        hn = rmsnorm(h, g[0])
        if i % 2 == 0:
            m = rwkv_pool_mixer(hn, ev_w_in[j], ev_mu[j], ev_w0[j], ev_w_up[j], ev_a0[j],
                                ev_a_up[j], ev_g_up[j], ev_k_k[j], ev_k_a[j], ev_r_k[j],
                                ev_ln_w[j], ev_ln_b[j], ev_pool_w[j], ev_pool_scale[j], ev_w_out[j])
        else:
            m = diff_attn_mixer(hn, od_w_in[j], od_lambda[j], od_subln_w[j], od_w_out[j], cos, sin, i)
        h = h + rmsnorm(m, g[1])
        f = sq_relu_mlp(rmsnorm(h, g[2]), mlp_w1[i], mlp_w2[i])
        h = h + rmsnorm(f, g[3])
    return h[:, N_META:]


def setup_inputs(seed=0):
    out = dict(first_inputs(seed))
    for name, value in second_inputs(seed + 1).items():
        if name != "x":
            out[name + "_2"] = value
    return out


def reference(
    x, mem, norm_w, mem_norm_w, gla_w_in, gla_w_gate_up, gla_gate_bias, gla_out_norm_w, s5_w_in,
    s5_lam_re, s5_lam_im, s5_log_step, s5_b_re, s5_b_im, s5_c_re, s5_c_im, s5_d, s5_w_glu,
    s5_b_glu, xa_w_kv, w_out, final_norm_w, meta_2, norm_g_2, mlp_w1_2, mlp_w2_2, ev_w_in_2,
    ev_mu_2, ev_w0_2, ev_w_up_2, ev_a0_2, ev_a_up_2, ev_g_up_2, ev_k_k_2, ev_k_a_2, ev_r_k_2,
    ev_ln_w_2, ev_ln_b_2, ev_pool_w_2, ev_pool_scale_2, ev_w_out_2, od_w_in_2, od_lambda_2,
    od_subln_w_2, od_w_out_2,
):
    x = first_block(
        x, mem, norm_w, mem_norm_w, gla_w_in, gla_w_gate_up, gla_gate_bias, gla_out_norm_w,
        s5_w_in, s5_lam_re, s5_lam_im, s5_log_step, s5_b_re, s5_b_im, s5_c_re, s5_c_im, s5_d,
        s5_w_glu, s5_b_glu, xa_w_kv, w_out, final_norm_w,
    )
    return second_block(
        x, meta_2, norm_g_2, mlp_w1_2, mlp_w2_2, ev_w_in_2, ev_mu_2, ev_w0_2, ev_w_up_2,
        ev_a0_2, ev_a_up_2, ev_g_up_2, ev_k_k_2, ev_k_a_2, ev_r_k_2, ev_ln_w_2, ev_ln_b_2,
        ev_pool_w_2, ev_pool_scale_2, ev_w_out_2, od_w_in_2, od_lambda_2, od_subln_w_2,
        od_w_out_2,
    )


_drawn_inputs = setup_inputs


def setup_inputs(seed=0):
    import zlib

    import numpy as np

    out = dict(_drawn_inputs(seed))
    spreads = {}
    factors = {'mem_norm_w': 8.0,
     'gla_out_norm_w': 5.205,
     's5_lam_re': 200.0,
     's5_b_glu': 200.0,
     'ev_w_up_2': 3.386,
     'ev_a0_2': 3.536,
     'ev_k_k_2': 189.359,
     'ev_ln_b_2': 3.459,
     's5_lam_im': 64.0,
     's5_log_step': 64.0,
     's5_b_re': 64.0,
     's5_b_im': 64.0,
     's5_c_re': 64.0,
     's5_c_im': 64.0,
     's5_w_glu': 3.637}
    for name, (base, spread) in spreads.items():
        noise = np.random.default_rng([zlib.crc32(name.encode()), seed]).standard_normal(out[name].shape)
        drawn = base * np.exp(spread * noise) if base else spread * noise
        out[name] = __import__('jax').numpy.asarray(drawn.astype(out[name].dtype))
    for name, factor in factors.items():
        out[name] = (out[name] * factor).astype(out[name].dtype)
    return out
```

```python
from contextlib import ExitStack

import numpy as np

import concourse.bass as bass
from concourse import mybir

ALU = mybir.AluOpType
ACT = mybir.ActivationFunctionType
AX = mybir.AxisListType
F32 = mybir.dt.float32
F32R = mybir.dt.float32r
I32 = mybir.dt.int32

P = 128
D = 1024
KD = D // P
L1 = 512
META = 16
L2 = L1 + META
N_MEM = 256
EPS = 1e-6
SEQ_W = 2 * D
XA_HEADS = 4
XA_DIM = D // XA_HEADS
MIX = SEQ_W + D
GLA_HEADS = 4
DK = (D // 2) // GLA_HEADS
DV = SEQ_W // GLA_HEADS
RANK = 16
TAU = 16.0
CHUNK = 64
RING = 4
UNIT = 1024
FULL = [(0, L1)]
HALVES = [(0, L2 // 2), (L2 // 2, L2 // 2)]
MEMS = [(0, N_MEM)]
ARENA = 33600


class Chain:

    def __init__(self, eng, sem):
        self.eng, self.sem, self.n = eng, sem, 0

    def link(self, ins):
        self.n += 1
        ins.then_inc(self.sem, 1)
        self.eng.wait_ge(self.sem, self.n)


class Board:

    def __init__(self, nc, ctx):
        self.nc, self.ctx = nc, ctx
        self.units = 0
        self.full = [0, 0]
        self.last_rms = None

    def sem(self, name):
        return self.ctx.enter_context(self.nc.semaphore(name))

    def sb(self, name, shape, dt=F32):
        return self.ctx.enter_context(self.nc.sbuf_tensor(name, shape, dt))

    def sb_both(self, name, shape):
        with self.nc.sbuf_tensor(name, shape, F32) as plain:
            pass
        return plain, self.sb(name + "_r", shape, F32R)


class Stage:

    def tensor(self, pe):
        pass

    def scalar(self, act):
        pass

    def vector(self, dve):
        pass

    def gpsimd(self, pool):
        pass


class Gemm(Stage):

    def __init__(self, b, name, kind, x, kt, outs, ranges, store, engines, needs, tiles=None, before=None,
                 high=None, x_hi=None, after=None, ready=None):
        self.ready = ready
        self.fed = False
        self.after = after
        self.b, self.name, self.kind, self.x, self.kt = b, name, kind, x, kt
        self.ranges, self.store, self.engines, self.needs = ranges, store, engines, needs
        self.tiles, self.before = tiles, before
        if kind == "fm":
            self.per_out = kt // 8
            self.slots = 4 if len(ranges) == 1 else 2
            self.body_outs = self.slots
            while self.body_outs * self.per_out % RING:
                self.body_outs += self.slots
            if outs < self.body_outs or outs % self.body_outs:
                self.body_outs = outs
            self.body_units = self.body_outs * self.per_out
            self.iters = outs // self.body_outs
            self.pars = [o % 2 for o in range(self.body_outs)]
        else:
            self.body_units = kt // 2
            self.body_outs = len(tiles)
            self.slots = len(tiles)
            self.iters = outs
            self.pars = [i % 2 for i in range(len(tiles))]
        self.unit0 = b.units
        self.full0 = list(b.full)
        self.body_par = [self.pars.count(0), self.pars.count(1)]
        self.peel = min(self.full0) == 0 or self.iters == 1 or before is not None or high is not None
        self.high, self.x_hi, self.split0 = high, x_hi, b.splits
        if high is not None:
            assert self.body_units % 2 == 0, name
            b.splits += self.body_units * self.iters
        b.units += self.body_units * self.iters
        b.full = [f + self.iters * n for f, n in zip(b.full, self.body_par)]
        self.done = list(b.full)
        if self.iters > 1:
            assert self.body_units % RING == 0, name

    def tile(self, m):
        return self.b.stored[m % 2], self.full0[m % 2] + m // 2 + 1

    def bank(self, o):
        if self.kind == "tm":
            return [self.b.ps[:, o, :]]
        n = len(self.ranges)
        s = o % self.slots
        return [self.b.ps[:, s * n + r, 0:w] for r, (_, w) in enumerate(self.ranges)]

    def loop(self, eng, body):
        if self.high is not None and (self.iters == 2 or self.after):
            for it in range(self.iters):
                body(it)
            return
        if self.peel:
            body(0)
        if self.iters > self.peel:
            with eng.Fori(int(self.peel), self.iters) as it:
                body(it)

    def unit(self, pe, it, j):
        u = self.unit0 + j
        if self.high is not None:
            pe.wait_ge(self.b.unit_lo, self.split0 + j + 1 + it * self.body_units)
            return self.b.ring_r[:, u % RING, :]
        pe.wait_ge(self.b.landed[u % RING], 16 * (u // RING + 1) + it * (16 * (self.body_units // RING)))
        return self.b.ring[:, u % RING, :]

    def count(self, o, it):
        par = self.pars[o % self.body_outs]
        n = self.pars[:o % self.body_outs + 1].count(par)
        if o < 0:
            n -= self.body_par[par]
        return par, self.full0[par] + n + it * self.body_par[par]

    def tensor(self, pe):
        b, mm = self.b, self.b.nc.tensor.matmul
        for s, v in self.needs:
            pe.wait_ge(s, v)
        for par in range(2):
            if self.full0[par]:
                pe.wait_ge(b.stored[par], self.full0[par])

        def free(o, it):
            if not (isinstance(it, int) and it == 0 and o < self.slots):
                par, n = self.count(o - self.slots, it)
                pe.wait_ge(b.stored[par], n)

        def feature_major(it):
            for o in range(self.body_outs):
                free(o, it)
                for c in range(self.per_out):
                    w = self.unit(pe, it, o * self.per_out + c)
                    for k in range(8 * c, 8 * c + 8):
                        if self.high is not None:
                            if self.ready and o == 0 and isinstance(it, int) and it == 0:
                                pe.wait_ge(*self.ready(k))
                            cols, hi = slice(k % 8 * P, (k % 8 + 1) * P), self.high[:, (o * self.per_out + c) % 2, :]
                            for acc, (t0, tn) in zip(self.bank(o), self.ranges):
                                part = mm(acc, hi[:, cols], self.x_hi(k)[:, t0:t0 + tn], start=(k == 0), stop=False)
                                if k % 8 == 0 and t0 == 0:
                                    part.then_inc(b.begun, 1)
                                mm(acc, hi[:, cols], self.x(k)[:, t0:t0 + tn], start=False, stop=False)
                            for acc, (t0, tn) in zip(self.bank(o), self.ranges):
                                ins = mm(acc, w[:, cols], self.x_hi(k)[:, t0:t0 + tn], start=False, stop=(k == self.kt - 1))
                            continue
                        for acc, (t0, tn) in zip(self.bank(o), self.ranges):
                            ins = mm(acc, w[:, k % 8 * P:(k % 8 + 1) * P], self.x(k)[:, t0:t0 + tn],
                                     start=(k == 0), stop=(k == self.kt - 1))
                            if k % 8 == 0 and t0 == 0:
                                ins.then_inc(b.begun, 1)
                ins.then_inc(b.filled[self.pars[o]], 1)

        def token_major(it):
            for j in range(self.body_units):
                w = self.unit(pe, it, j).rearrange("p (k n) -> p k n", k=2)
                for i, (t0, tn) in enumerate(self.tiles):
                    if j == 0:
                        free(i, it)
                    for kk in range(2):
                        if self.high is not None:
                            hi = self.high[:, j % 2, kk * 512:kk * 512 + 512]
                            out, k, tok = b.ps[0:tn, i, :], 2 * j + kk, slice(t0, t0 + tn)
                            part = mm(out, self.x_hi(k)[:, tok], hi, start=(k == 0), stop=False)
                            if i == 0 and kk == 0:
                                part.then_inc(b.begun, 1)
                            mm(out, self.x_hi(k)[:, tok], w[:, kk, :], start=False, stop=False)
                            ins = mm(out, self.x(k)[:, tok], hi, start=False, stop=(k == self.kt - 1))
                            continue
                        ins = mm(b.ps[0:tn, i, :], self.x(2 * j + kk)[:, t0:t0 + tn], w[:, kk, :],
                                 start=(j + kk == 0), stop=(2 * j + kk == self.kt - 1))
                        if i == 0 and kk == 0:
                            ins.then_inc(b.begun, 1)
                    if j == self.body_units - 1:
                        ins.then_inc(b.filled[self.pars[i]], 1)

        self.loop(pe, feature_major if self.kind == "fm" else token_major)

    def make_high(self, act, j, it):
        b, u = self.b, self.unit0 + j
        act.wait_ge(b.landed[u % RING], 16 * (u // RING + 1) + it * (16 * (self.body_units // RING)))
        act.wait_ge(b.begun, u + it * self.body_units)
        b.nc.scalar.activation(self.high[:, j % 2, :], b.ring[:, u % RING, :], ACT.Copy).then_inc(b.unit_hi, 1)

    def evacuate(self, eng, which):
        if which not in self.engines:
            return

        def body(it):
            for o in range(self.body_outs):
                if self.engines[self.pars[o]] != which:
                    continue
                par, n = self.count(o, it)
                eng.wait_ge(self.b.filled[par], n)
                if self.before and not (isinstance(it, int) and it == 0):
                    self.before(eng, o, it)
                if self.kind == "fm":
                    self.store(which, it * self.body_outs + o, self.bank(o), o).then_inc(self.b.stored[par], 1)
                else:
                    part = self.b.ps[0:self.tiles[o][1], o, :]
                    self.store(which, (it, o), part, o).then_inc(self.b.stored[par], 1)
        self.loop(eng, body)

    def scalar(self, act):
        if self.high is None:
            self.evacuate(act, "act")
            return
        b = self.b
        for sem, v in self.needs:
            act.wait_ge(sem, v)
        last = self.body_units - 1

        def evacuate(q, it, back):
            if self.kind == "fm":
                outs = [q // self.per_out] if q % self.per_out == self.per_out - 1 else []
            else:
                outs = range(self.body_outs) if q == last else []
            for o in outs:
                if self.engines[self.pars[o]] != "act":
                    continue
                par, n = self.count(o - self.body_outs if back else o, it)
                act.wait_ge(b.filled[par], n)
                if self.before and it - back > 0:
                    self.before(act, o, it - back)
                if self.kind == "fm":
                    m = it * self.body_outs + (o - self.body_outs if back else o)
                    self.store("act", m, self.bank(o), o).then_inc(b.stored[par], 1)
                    if self.after:
                        self.after(act, m, o, par, n)
                else:
                    part = b.ps[0:self.tiles[o][1], o, :]
                    self.store("act", (it - 1 if back else it, o), part, o).then_inc(b.stored[par], 1)

        def body(it):
            for j in range(self.body_units):
                if not (self.fed and isinstance(it, int) and it + j == 0):
                    self.make_high(act, j, it)
                if j:
                    evacuate(j - 1, it, False)
                elif not (isinstance(it, int) and it == 0):
                    evacuate(last, it, True)

        self.loop(act, body)
        evacuate(last, self.iters - 1, False)

    def gpsimd(self, pool):
        if self.high is None:
            return
        b = self.b

        def body(it):
            for j in range(self.body_units):
                slot = (self.unit0 + j) % RING
                pool.wait_ge(b.unit_hi, self.split0 + j + 1 + it * self.body_units)
                b.nc.gpsimd.tensor_tensor(b.ring_r[:, slot, :], b.ring[:, slot, :], self.high[:, j % 2, :],
                                          ALU.subtract).then_inc(b.unit_lo, 1)
        self.loop(pool, body)

    def vector(self, dve):
        self.evacuate(dve, "dve")


class Rms(Stage):

    def __init__(self, b, x, n, ranges, width, eps, w, out, banks, needs, stay=(), view=None, onto=None,
                 hi=None, lo=None, each=None):
        self.each = each
        self.b, self.x, self.n, self.ranges, self.width = b, x, n, ranges, width
        self.eps, self.w, self.out, self.banks, self.needs, self.stay = eps, w, out, banks, needs, stay
        self.view = view or (lambda ap: ap)
        self.onto = onto
        self.at = dict(b.norms)
        self.tokens = sum(w for _, w in ranges)
        b.norms["squared"] += n
        b.norms["summed"] += n
        b.norms["rooted"] += len(ranges)
        b.norms["inverted"] += 1
        b.norms["ready"] += n
        self.rooted = (b.rooted, b.norms["rooted"])
        self.ready = (b.normed, b.norms["ready"])
        self.tile = lambda k: (b.normed, self.at["ready"] + k + 1)
        if onto:
            self.tile = lambda k: (b.summed_onto, self.at["summed_onto"] + k + 1)
            b.norms["summed_onto"] += n
            self.ready = (b.summed_onto, b.norms["summed_onto"])
        self.feeds = None
        self.hi, self.lo = hi, lo
        if hi:
            b.norms["parts"] += n
            self.ready = (b.out_lo, b.norms["parts"])

    def scalar(self, act):
        b, at = self.b, self.at
        for s, v in self.needs:
            act.wait_ge(s, v)
        for k in range(self.n):
            if self.each:
                act.wait_ge(*self.each(k))
            if k >= 2:
                act.wait_ge(b.summed, at["summed"] + k - 1)
            b.nc.scalar.activation(b.sq[:, k % 2, 0:self.tokens], self.x(k), ACT.Square).then_inc(b.squared, 1)
        act.wait_ge(b.summed, at["summed"] + self.n)
        if at["inverted"]:
            act.wait_ge(b.inverted, at["inverted"])
        for bank, (t0, tn) in zip(self.banks, self.ranges):
            b.nc.scalar.activation(b.root[:, t0:t0 + tn], b.ps[:, bank, 0:tn], ACT.Sqrt,
                                   bias=b.eps[self.eps], scale=1.0 / self.width).then_inc(b.rooted, 1)
        if self.feeds:
            self.feeds.make_high(act, 0, 0)
        for k in range(self.n if self.hi else 0):
            act.wait_ge(b.normed, at["ready"] + k + 1)
            b.nc.scalar.activation(self.hi(k), self.out(k), ACT.Copy).then_inc(b.out_hi, 1)

    def tensor(self, pe):
        b, at = self.b, self.at
        for s, v in self.stay:
            pe.wait_ge(s, v)
        for k in range(self.n):
            pe.wait_ge(b.squared, at["squared"] + k + 1)
            for bank, (t0, tn) in zip(self.banks, self.ranges):
                ins = b.nc.tensor.matmul(b.ps[:, bank, 0:tn], b.ones[:, :], b.sq[:, k % 2, t0:t0 + tn],
                                         start=(k == 0), stop=(k == self.n - 1))
            ins.then_inc(b.summed, 1)

    def vector(self, dve):
        b, at = self.b, self.at
        dve.wait_ge(*self.rooted)
        if at["ready"]:
            dve.wait_ge(b.normed, at["ready"])
        b.nc.vector.reciprocal(b.inv[:, 0:self.tokens], b.root[:, 0:self.tokens]).then_inc(b.inverted, 1)
        dve.wait_ge(b.inverted, at["inverted"] + 1)
        for k in range(self.n + 2):
            if self.onto and 1 <= k <= self.n:
                dve.wait_ge(b.normed, at["ready"] + k)
                b.nc.vector.tensor_tensor(self.onto(k - 1), self.onto(k - 1), self.out(k - 1),
                                          ALU.add).then_inc(b.summed_onto, 1)
            if k < self.n:
                b.nc.vector.scalar_tensor_tensor(
                    out=self.out(k), in0=self.view(self.x(k)), scalar=self.w(k),
                    in1=self.view(b.inv[:, 0:self.tokens]), op0=ALU.mult, op1=ALU.mult).then_inc(b.normed, 1)
            if self.hi and k >= 2:
                dve.wait_ge(b.out_hi, at["parts"] + k - 1)
                b.nc.vector.tensor_tensor(self.lo(k - 2), self.out(k - 2), self.hi(k - 2),
                                          ALU.subtract).then_inc(b.out_lo, 1)
        if self.onto:
            dve.wait_ge(*self.ready)


    def feed(self, gemm):
        gemm.ready = lambda k: (self.b.out_lo, self.at["parts"] + k + 1)
        gemm.needs, gemm.fed, self.feeds = [], True, gemm


class MemoryAttention(Stage):

    def __init__(self, b, name, q, k, v, z, needs):
        self.b, self.q, self.k, self.v, self.z, self.needs = b, q, k, v, z, needs
        self.steps = XA_HEADS * 4
        self.s0, self.o0 = b.attentions * self.steps, b.attentions * 2 * XA_HEADS
        b.attentions += 1
        (self.scored, self.maxed, self.powered, self.inverse, self.scaled, self.turned, self.kept,
         self.mixed, self.gated) = b.attention_sems
        self.done = (self.gated, self.o0 + 2 * XA_HEADS)

    def tensor(self, pe):
        b = self.b
        for s, v in self.needs:
            pe.wait_ge(s, v)
        for n in range(self.steps + 2):
            if n < self.steps:
                h, t = divmod(n, 4)
                if n >= 2:
                    pe.wait_ge(self.powered, self.s0 + n - 1)
                for c in range(2):
                    ins = b.nc.tensor.matmul(b.ps[:, 4 + n % 2, 0:N_MEM], self.q(2 * h + c)[:, t * P:(t + 1) * P],
                                             self.k(2 * h + c), start=(c == 0), stop=(c == 1))
                ins.then_inc(self.scored, 1)
            if n >= 2 and (n - 2) % 4 == 3:
                h = (n - 2) // 4
                pe.wait_ge(self.kept, self.s0 + 4 * h + 4)
                for c in range(2):
                    if h >= 1:
                        pe.wait_ge(self.gated, self.o0 + 2 * h - 1 + c)
                    for m in range(2):
                        ins = b.nc.tensor.matmul(b.ps[:, 6 + c, :], self.v[:, m, (2 * h + c) * P:(2 * h + c + 1) * P],
                                                 b.pt[:, h % 2, m, :], start=(m == 0), stop=(m == 1))
                    ins.then_inc(self.mixed, 1)
            if 1 <= n <= self.steps:
                m = n - 1
                pe.wait_ge(self.scaled, self.s0 + m + 1)
                if m >= 2:
                    pe.wait_ge(self.kept, self.s0 + m - 1)
                for c in range(2):
                    ins = b.nc.tensor.transpose(b.ps[:, 2 + m % 2, c * P:(c + 1) * P],
                                                b.p[:, m % 2, c * P:(c + 1) * P], b.ident[:, :])
                ins.then_inc(self.turned, 1)

    def scalar(self, act):
        b = self.b
        for n in range(self.steps + 1):
            if n < self.steps:
                act.wait_ge(self.maxed, self.s0 + n + 1)
                if n >= 2:
                    act.wait_ge(self.turned, self.s0 + n - 1)
                b.nc.scalar.activation(b.p[:, n % 2, :], b.ps[:, 4 + n % 2, 0:N_MEM], ACT.Exp,
                                       bias=b.negmax[:, n % 2:n % 2 + 1],
                                       accum_out=b.total[:, n % 2:n % 2 + 1]).then_inc(self.powered, 1)
            if n >= 1:
                h, t = divmod(n - 1, 4)
                act.wait_ge(self.turned, self.s0 + n)
                if h >= 2:
                    act.wait_ge(self.mixed, self.o0 + 2 * h - 2)
                b.nc.scalar.activation(b.pt[:, h % 2, :, t * P:(t + 1) * P],
                                       b.ps[:, 2 + (n - 1) % 2, 0:2 * P].rearrange("p (c t) -> p c t", c=2),
                                       ACT.Copy).then_inc(self.kept, 1)

    def vector(self, dve):
        b = self.b
        for n in range(self.steps + 3):
            if n < self.steps:
                dve.wait_ge(self.scored, self.s0 + n + 1)
                if n >= 2:
                    dve.wait_ge(self.powered, self.s0 + n - 1)
                b.nc.vector.tensor_reduce(b.negmax[:, n % 2:n % 2 + 1], b.ps[:, 4 + n % 2, 0:N_MEM], AX.X, ALU.max,
                                          negate=True).then_inc(self.maxed, 1)
            if 1 <= n <= self.steps:
                c = (n - 1) % 2
                dve.wait_ge(self.powered, self.s0 + n)
                b.nc.vector.reciprocal(b.total[:, 2 + c:3 + c], b.total[:, c:c + 1]).then_inc(self.inverse, 1)
                dve.wait_ge(self.inverse, self.s0 + n)
                b.nc.vector.tensor_scalar(b.p[:, c, :], b.p[:, c, :], b.total[:, 2 + c:3 + c], None,
                                          ALU.mult).then_inc(self.scaled, 1)
            if n >= 3 and (n - 3) % 4 == 3:
                h = (n - 3) // 4
                for c in range(2):
                    dve.wait_ge(self.mixed, self.o0 + 2 * h + c + 1)
                    z = self.z(2 * h + c)
                    b.nc.vector.tensor_tensor(z, z, b.ps[:, 6 + c, :], ALU.mult).then_inc(self.gated, 1)


class Gla(Stage):

    def __init__(self, b, m, needs):
        self.b, self.m, self.needs = b, m, needs
        self.ranked = b.sem("gla_ranked")
        self.rank_kept = b.sem("gla_rank_kept")
        self.gated_in = b.sem("gla_gated_in")
        self.biased = b.sem("gla_biased")
        self.pre = b.sem("gla_pre")
        self.summed_up = b.sem("gla_summed_up")
        self.exped = b.sem("gla_exped")
        self.decayed = b.sem("gla_decayed")
        self.attended = b.sem("gla_attended")
        self.masked = b.sem("gla_masked")
        self.turned = b.sem("gla_turned")
        self.token_keys = b.sem("gla_token_keys")
        self.grown = b.sem("gla_grown")
        self.stated = b.sem("gla_stated")
        self.mixed = b.sem("gla_mixed")
        self.saved = b.sem("gla_saved")
        self.multiplied = b.sem("gla_multiplied")
        self.cleared = b.sem("gla_cleared")
        self.steps = GLA_HEADS * 4
        self.rms = []
        for h in range(GLA_HEADS):
            o = m.o[h % 2]
            self.rms.append(Rms(b, lambda k, o=o: o[:, k, :], DV // P, FULL, DV, EPS,
                                lambda k: b.col("gla_out_norm_w", k), lambda k, o=o: o[:, k, :], [0],
                                [(self.saved, 4 * h + 4)], [(self.masked, min(4 * h + 5, self.steps))]))
        self.done = (self.multiplied, 4 * GLA_HEADS)

    def tensor(self, pe):
        b, m, mm = self.b, self.m, self.b.nc.tensor.matmul
        for s, v in self.needs:
            pe.wait_ge(s, v)
        for k in range(KD):
            for part, h in enumerate((b.h_hi, b.h_r)):
                ins = mm(b.ps[0:RANK, 5, :], m.w_rank[:, k, :], h[:, k, 0:L1].bitcast(F32), start=(k + part == 0),
                         stop=(k + part == KD))
        ins.then_inc(self.ranked, 1)
        pe.wait_ge(self.rank_kept, 1)
        for h in range(GLA_HEADS):
            if h >= 2:
                pe.wait_ge(self.biased, h - 1)
            mm(b.ps[:, 6 + h % 2, :], m.w_up[0:RANK, h * P:(h + 1) * P], m.rank[0:RANK, :],
               start=True, stop=True).then_inc(self.gated_in, 1)
        for n in range(self.steps + 2):
            if n < self.steps:
                h, t = divmod(n, 4)
                tok = slice(t * P, (t + 1) * P)
                pe.wait_ge(self.decayed, 4 * h + 4)
                if n >= 2:
                    pe.wait_ge(self.masked, n - 1)
                if n >= 6 and n % 4 == 2:
                    pe.wait_ge(*self.rms[(n - 6) // 4].rooted)
                mm(b.ps[:, n % 2, 0:P], m.k[:, h, tok], m.q[:, h, tok], start=True, stop=True).then_inc(self.attended, 1)
                if n >= 2:
                    pe.wait_ge(self.token_keys, n - 1)
                b.nc.tensor.transpose(b.ps[:, 2 + n % 2, 0:P], m.kend[:, h, tok], b.ident[:, :]).then_inc(self.turned, 1)
            if 1 <= n <= self.steps:
                j = n - 1
                h, t = divmod(j, 4)
                pe.wait_ge(self.token_keys, j + 1)
                for c in range(2):
                    if j >= 1:
                        pe.wait_ge(self.stated, 2 * j - 1 + c)
                    rows = slice(CHUNK * c, CHUNK * c + CHUNK)
                    mm(b.ps[:, 4 + c, :], m.ktok[rows, j % 2, :], m.v[rows, t, h * DV:(h + 1) * DV],
                       start=True, stop=True).then_inc(self.grown, 1)
                pe.wait_ge(self.masked, j + 1)
                if j >= 2:
                    pe.wait_ge(self.saved, j - 1)
                elif j == 0:
                    pe.wait_ge(self.biased, GLA_HEADS)
                pe.wait_ge(self.stated, 2 * j + 1)
                for e in range(4):
                    o = b.ps[:, 6 + j % 2, e * P:(e + 1) * P]
                    ins = mm(o, m.v[:, t, h * DV + e * P:h * DV + (e + 1) * P], m.att[:, j % 2, :],
                             start=True, stop=False)
                    for c in range(2):
                        if t + c:
                            cols = slice(t * P + CHUNK * c, t * P + CHUNK * c + CHUNK)
                            ins = mm(o[:, CHUNK * c:CHUNK * c + CHUNK],
                                     m.state[:, (2 * j + c) % 3, e * P:(e + 1) * P], m.q[:, h, cols],
                                     start=False, stop=(c == 1))
                ins.then_inc(self.mixed, 1)
            if n >= 5 and n % 4 == 1:
                self.rms[(n - 5) // 4].tensor(pe)

    def scalar(self, act):
        b, m = self.b, self.m
        act.wait_ge(self.ranked, 1)
        b.nc.scalar.activation(m.rank[0:RANK, :], b.ps[0:RANK, 5, :], ACT.Copy).then_inc(self.rank_kept, 1)
        for h in range(GLA_HEADS):
            act.wait_ge(self.gated_in, h + 1)
            b.nc.scalar.activation(m.kend[:, h, :], b.ps[:, 6 + h % 2, :], ACT.Identity,
                                   bias=b.col("gla_gate_bias", h)).then_inc(self.biased, 1)

        def gate(h):
            act.wait_ge(self.pre, 2 * h + 2)
            b.nc.scalar.activation(m.t_exp, m.t_neg, ACT.Exp).then_inc(self.exped, 1)
            act.wait_ge(self.exped, 5 * h + 1)
            b.nc.scalar.activation(m.t_log, m.t_exp, ACT.Ln, bias=1.0).then_inc(self.exped, 1)
            act.wait_ge(self.summed_up, 3 * h + 3)
            if h:
                act.wait_ge(self.decayed, 4 * h)
            b.nc.scalar.activation(m.e_pos, m.t_cum, ACT.Exp, scale=1 / TAU).then_inc(self.exped, 1)
            b.nc.scalar.activation(m.e_neg, m.t_cum, ACT.Exp, scale=-1 / TAU).then_inc(self.exped, 1)
            b.nc.scalar.activation(m.e_end, m.t_end, ACT.Exp, scale=1 / TAU).then_inc(self.exped, 1)

        gate(0)
        for n in range(self.steps + 2):
            if n % 4 == 0 and n // 4 + 1 < GLA_HEADS:
                gate(n // 4 + 1)
            if n < self.steps:
                act.wait_ge(self.turned, n + 1)
                if n >= 2:
                    act.wait_ge(self.grown, 2 * n - 2)
                b.nc.scalar.activation(m.ktok[:, n % 2, :], b.ps[:, 2 + n % 2, 0:P], ACT.Copy).then_inc(self.token_keys, 1)
            if 1 <= n <= self.steps:
                j = n - 1
                h, t = divmod(j, 4)
                act.wait_ge(self.mixed, j + 1)
                if h >= 2:
                    act.wait_ge(self.multiplied, 4 * (h - 1))
                b.nc.scalar.activation(m.o[h % 2][:, :, t * P:(t + 1) * P],
                                       b.ps[:, 6 + j % 2, :].rearrange("p (e t) -> p e t", e=4),
                                       ACT.Copy).then_inc(self.saved, 1)
            if n >= 5 and n % 4 == 1:
                self.rms[(n - 5) // 4].scalar(act)

    def vector(self, dve):
        b, m, v = self.b, self.m, self.b.nc.vector
        v.memset(m.att[:, :, :], 0.0).then_inc(self.cleared, 1)
        dve.wait_ge(self.cleared, 1)

        def gate(h):
            dve.wait_ge(self.biased, h + 1)
            v.tensor_scalar(m.t_min, m.kend[:, h, :], 0.0, None, ALU.min).then_inc(self.pre, 1)
            dve.wait_ge(self.pre, 2 * h + 1)
            v.scalar_tensor_tensor(out=m.t_neg, in0=m.t_min, scalar=2.0, in1=m.kend[:, h, :], op0=ALU.mult,
                                   op1=ALU.subtract).then_inc(self.pre, 1)
            dve.wait_ge(self.exped, 5 * h + 2)
            v.tensor_tensor(m.t_a, m.t_min, m.t_log, ALU.subtract).then_inc(self.summed_up, 1)
            dve.wait_ge(self.summed_up, 3 * h + 1)
            v.tensor_tensor_scan(m.t_cum, b.restart64[:, :], m.t_a, 0.0, ALU.mult, ALU.add).then_inc(self.summed_up, 1)
            dve.wait_ge(self.summed_up, 3 * h + 2)
            cum = m.t_cum.rearrange("p (c t) -> p c t", t=CHUNK)
            v.tensor_tensor(m.t_end.rearrange("p (c t) -> p c t", t=CHUNK),
                            cum[:, :, CHUNK - 1:CHUNK].broadcast_to([P, L1 // CHUNK, CHUNK]), cum,
                            ALU.subtract).then_inc(self.summed_up, 1)
            dve.wait_ge(self.exped, 5 * h + 5)
            q, k = m.q[:, h, :], m.k[:, h, :]
            v.scalar_tensor_tensor(out=q, in0=q, scalar=float(np.float32(DK ** -0.5)), in1=m.e_pos, op0=ALU.mult,
                                   op1=ALU.mult).then_inc(self.decayed, 1)
            v.tensor_tensor(m.kend[:, h, :], k, m.e_end, ALU.mult).then_inc(self.decayed, 1)
            v.tensor_copy(m.decay[:, h, :], m.e_pos.rearrange("p (c t) -> p c t", t=CHUNK)[:, :, CHUNK - 1]
                          ).then_inc(self.decayed, 1)
            v.tensor_tensor(k, k, m.e_neg, ALU.mult).then_inc(self.decayed, 1)
            dve.wait_ge(self.decayed, 4 * h + 4)

        gate(0)
        for n in range(self.steps + 3):
            if n % 4 == 0 and n // 4 + 1 < GLA_HEADS:
                gate(n // 4 + 1)
            if n < self.steps:
                dve.wait_ge(self.attended, n + 1)
                if n >= 2:
                    dve.wait_ge(self.mixed, n - 1)
                v.copy_predicated(m.att[:, n % 2, :], b.causal64[:, :].bitcast(I32),
                                  b.ps[:, n % 2, 0:P]).then_inc(self.masked, 1)
            if 1 <= n <= self.steps:
                j = n - 1
                h, t = divmod(j, 4)
                for c in range(2):
                    i = 2 * j + c
                    dve.wait_ge(self.grown, i + 1)
                    if j:
                        dve.wait_ge(self.mixed, j)
                    if i:
                        dve.wait_ge(self.stated, i)
                    new, ps = m.state[:, (i + 1) % 3, :], b.ps[:, 4 + c, :]
                    if t + c == 0:
                        v.tensor_copy(new, ps).then_inc(self.stated, 1)
                    else:
                        v.scalar_tensor_tensor(out=new, in0=m.state[:, i % 3, :], scalar=m.decay[:, h, 2 * t + c:2 * t + c + 1],
                                               in1=ps, op0=ALU.mult, op1=ALU.add).then_inc(self.stated, 1)
            if n >= 6 and n % 4 == 2:
                h = (n - 6) // 4
                rms = self.rms[h]
                rms.vector(dve)
                for k in range(4):
                    dve.wait_ge(b.normed, rms.at["ready"] + k + 1)
                    z = m.z[:, 4 * h + k, :]
                    v.tensor_tensor(z, z, m.o[h % 2][:, k, :], ALU.mult).then_inc(self.multiplied, 1)


S5_G = 128
S5_P = 64
S5_H = 16
S5_C = 8
S5_J = L1 // S5_C
NB = S5_G // 8
MAGIC = 12582912.0
TWO_PI = (6.28125, 0.001934051513671875, 2 * np.pi - 6.28125 - 0.001934051513671875)


class S5Tables(Stage):

    def __init__(self, b, m, a, needs):
        self.b, self.m, self.a, self.needs = b, m, a, needs
        self.fetched = b.sem("s5t_fetched")
        self.waved = b.sem("s5t_waved")
        self.phased = b.sem("s5t_phased")
        self.q_ready = b.sem("s5t_q_ready")
        self.q_stored = b.sem("s5t_q_stored")
        self.block_in = [b.sem("s5t_in_even"), b.sem("s5t_in_odd")]
        self.block_out = [b.sem("s5t_out_even"), b.sem("s5t_out_odd")]
        self.made = b.sem("s5t_made")
        self.prepared = b.sem("s5t_prepared")
        self.inner = b.sem("s5t_inner")
        self.done = [(self.block_out[c], 32 * NB // 2) for c in range(2)]

    def load(self, pool, m_, par):
        b, m, a = self.b, self.m, self.a
        s = self.block_in[par]
        pool.dma_start(m.cin[par], a["s5_c"][m_]).then_inc(s, 16)
        pool.dma_start(m.bin[par], a["s5_ba"][m_]).then_inc(s, 16)
        pool.dma_start(m.bk[par], a["s5_bk"][m_].unsqueeze(0).broadcast_to([S5_C, S5_H, 2, 512])).then_inc(s, 16)
        q = b.d_q.rearrange("c k (m n) -> m k c n", m=NB)[m_]
        for c in range(2):
            pool.dma_start(m.qk[par][:, c], q[:, c].unsqueeze(1).broadcast_to([S5_C, S5_H, 512])).then_inc(s, 16)

    LOADS = 5

    def gpsimd(self, pool):
        b, m, a = self.b, self.m, self.a
        pool.dma_start(m.par[:, 0:3, :], a["s5_par"]).then_inc(self.fetched, 16)
        for s, v in self.needs:
            pool.wait_ge(s, v)
        pool.wait_ge(self.q_ready, 1)
        pool.dma_start(b.d_q.rearrange("c k (g p) -> g c k p", g=S5_G), m.q).then_inc(self.q_stored, 16)
        pool.wait_ge(self.q_stored, 16)
        pool.wait_ge(self.prepared, 1)

        def store(m_, par):
            pool.dma_start(b.d_ca[m_], m.ca[par]).then_inc(self.block_out[par], 16)
            pool.dma_start(b.d_pb[m_], m.pb[par]).then_inc(self.block_out[par], 16)

        for par in range(2):
            self.load(pool, par, par)
        with pool.Fori(0, NB // 2 - 1) as it:
            for par in range(2):
                pool.wait_ge(self.made, it * 2 + par + 1)
                store(it * 2 + par, par)
                self.load(pool, it * 2 + par + 2, par)
        for par in range(2):
            pool.wait_ge(self.made, NB - 1 + par)
            store(NB - 2 + par, par)

    def scalar(self, act):
        b, w = self.b, self.m.par
        f = b.nc.scalar.activation
        act.wait_ge(self.fetched, 16)
        f(w[:, 3, :], w[:, 2, :], ACT.Exp).then_inc(self.waved, 1)
        act.wait_ge(self.phased, 1)
        f(w[:, 5, :], w[:, 4, :], ACT.Exp).then_inc(self.waved, 1)
        act.wait_ge(self.phased, 2)
        f(w[:, 7, :], w[:, 6, :], ACT.Sin).then_inc(self.waved, 1)
        f(w[:, 8, :], w[:, 6, :], ACT.Sin, scale=0.5).then_inc(self.waved, 1)

    def vector(self, dve):
        b, m = self.b, self.m
        v, w = b.nc.vector, self.m.par
        link = b.chain.link
        tt, ts, stt = v.tensor_tensor, v.tensor_scalar, v.scalar_tensor_tensor
        lr, li, dt, x, mag, r, sn, sh, t, u, cr, ci = (w[:, i, :] for i in (0, 1, 3, 4, 5, 6, 7, 8, 9, 10, 11, 12))
        for s, n in self.needs:
            dve.wait_ge(s, n)
        dve.wait_ge(self.waved, 1)
        tt(x, lr, dt, ALU.mult).then_inc(self.phased, 1)
        link(tt(t, li, dt, ALU.mult))
        link(ts(u, t, 1 / (2 * np.pi), MAGIC, ALU.mult, ALU.add))
        link(ts(u, u, MAGIC, None, ALU.subtract))
        for c in TWO_PI:
            link(stt(out=t, in0=u, scalar=-float(c), in1=t, op0=ALU.mult, op1=ALU.add))
        ts(r, t, -3.1415925, 3.1415925, ALU.max, ALU.min).then_inc(self.phased, 1)
        dve.wait_ge(self.phased, 2)
        link(tt(t, lr, lr, ALU.mult))
        link(tt(u, li, li, ALU.mult))
        link(tt(t, t, u, ALU.add))
        link(v.reciprocal(dt, t))
        dve.wait_ge(self.waved, 4)
        link(tt(u, sh, sh, ALU.mult))
        link(ts(u, u, -2.0, 1.0, ALU.mult, ALU.add))
        pr = lambda n: m.pow[:, 0, n, :]
        pi = lambda n: m.pow[:, 1, n, :]
        v.memset(pr(0), 1.0)
        v.memset(pi(0), 0.0)
        link(tt(pr(1), mag, u, ALU.mult))
        link(tt(pi(1), mag, sn, ALU.mult))
        link(ts(r, pr(1), 1.0, None, ALU.subtract))
        link(tt(t, r, lr, ALU.mult))
        link(tt(u, pi(1), li, ALU.mult))
        link(tt(t, t, u, ALU.add))
        link(tt(cr, t, dt, ALU.mult))
        link(tt(t, pi(1), lr, ALU.mult))
        link(tt(u, r, li, ALU.mult))
        link(tt(t, t, u, ALU.subtract))
        link(tt(ci, t, dt, ALU.mult))
        for n in range(1, S5_C):
            link(tt(t, pr(n), pr(1), ALU.mult))
            link(tt(u, pi(n), pi(1), ALU.mult))
            link(tt(pr(n + 1), t, u, ALU.subtract))
            link(tt(t, pr(n), pi(1), ALU.mult))
            link(tt(u, pi(n), pr(1), ALU.mult))
            link(tt(pi(n + 1), t, u, ALU.add))
        one = slice(S5_G, S5_G + S5_P)
        powr, powi = m.pow[:, 0, 0:S5_C, one], m.pow[:, 1, 0:S5_C, one]
        wide = lambda ap: ap[:, one].unsqueeze(1).broadcast_to([P, S5_C, S5_P])
        tmp = m.tmp[:, 0:512].rearrange("p (n q) -> p n q", n=S5_C)
        link(tt(m.q[:, 0], powr, wide(cr), ALU.mult))
        link(tt(tmp, powi, wide(ci), ALU.mult))
        link(tt(m.q[:, 0], m.q[:, 0], tmp, ALU.subtract))
        link(tt(m.q[:, 1], powi, wide(cr), ALU.mult))
        link(tt(tmp, powr, wide(ci), ALU.mult))
        tt(m.q[:, 1], m.q[:, 1], tmp, ALU.add).then_inc(self.q_ready, 1)
        lo, hi, two = slice(0, S5_P), slice(S5_P, P), slice(0, S5_G)
        for rows, e, part, sign in ((lo, 0, 0, 1.0), (hi, 0, 1, -1.0), (lo, 1, 1, -1.0), (hi, 1, 0, -1.0)):
            link(ts(m.e[rows, e], m.pow[rows, part, :, two], sign, None, ALU.mult))
        for rows, f, src, sign in ((lo, 0, cr, 1.0), (hi, 0, ci, 1.0), (lo, 1, ci, -1.0), (hi, 1, cr, 1.0)):
            link(ts(m.f[rows, f], src[rows, two], sign, None, ALU.mult))
        link(v.tensor_copy(b.a8[:, 0, :], pr(S5_C)[:, two]))
        link(ts(b.a8[lo, 1, :], pi(S5_C)[lo, two], 1.0, None, ALU.mult))
        ts(b.a8[hi, 1, :], pi(S5_C)[hi, two], -1.0, None, ALU.mult).then_inc(self.prepared, 1)
        dve.wait_ge(self.prepared, 1)
        dve.wait_ge(self.q_stored, 16)

        INNER = 10

        def block(it, par):
            m_ = it * 2 + par
            done = [0]

            def inner(ins):
                done[0] += 1
                ins.then_inc(self.inner, 1)
                dve.wait_ge(self.inner, m_ * INNER + done[0])

            dve.wait_ge(self.block_in[par], it * (16 * self.LOADS) + 16 * self.LOADS)
            if not isinstance(it, int) or it > 0:
                dve.wait_ge(self.block_out[par], it * 32)
            ca = m.ca[par][:, :, 0:144].rearrange("p g (n h) -> p g n h", h=S5_H)
            tmp = m.tmp[:, 0:1152].rearrange("p (g n h) -> p g n h", n=9, h=S5_H)
            bb = m.ca[par][:, :, 144:160]
            small = m.tmp[:, 0:128].rearrange("p (g h) -> p g h", h=S5_H)
            ge = bass.ds(m_ * 8, 8)
            for c in range(2):
                e = m.e[:, c, :, ge].rearrange("p n g -> p g n").unsqueeze(3).broadcast_to([P, 8, 9, S5_H])
                cc = m.cin[par][:, c].rearrange("p (g h) -> p g h", h=S5_H).unsqueeze(2).broadcast_to([P, 8, 9, S5_H])
                ins = tt((ca, tmp)[c], e, cc, ALU.mult)
                inner(ins)
            inner(tt(ca, ca, tmp, ALU.add))
            for c in range(2):
                f = m.f[:, c, ge].unsqueeze(2).broadcast_to([P, 8, S5_H])
                bc = m.bin[par][:, c].rearrange("p (g h) -> p g h", h=S5_H)
                inner(tt((bb, small)[c], f, bc, ALU.mult))
            inner(tt(bb, bb, small, ALU.add))
            q, k = m.qk[par], m.bk[par]
            t512 = m.tmp[:, 0:512]
            pbv = m.pb[par].rearrange("p g (c q) -> p c g q", c=2)
            eight = lambda ap: ap.rearrange("p (g q) -> p g q", g=8)
            inner(tt(pbv[:, 0], eight(q[:, 0]), eight(k[:, 0]), ALU.mult))
            inner(tt(t512, q[:, 1], k[:, 1], ALU.mult))
            tt(pbv[:, 0], pbv[:, 0], eight(t512), ALU.subtract)
            inner(tt(pbv[:, 1], eight(q[:, 0]), eight(k[:, 1]), ALU.mult))
            inner(tt(t512, q[:, 1], k[:, 0], ALU.mult))
            tt(pbv[:, 1], pbv[:, 1], eight(t512), ALU.add).then_inc(self.made, 1)
            dve.wait_ge(self.made, m_ + 1)

        block(0, 0)
        block(0, 1)
        with dve.Fori(1, NB // 2) as it:
            for par in range(2):
                block(it, par)

    def tensor(self, pe):
        pass


class S5Inputs(Stage):

    def __init__(self, b, m, sent, needs):
        self.b, self.m, self.sent, self.needs = b, m, sent, needs
        self.u_in = b.sem("s5i_u_in")
        self.block_in = [b.sem("s5i_in_even"), b.sem("s5i_in_odd")]
        self.responded = b.sem("s5i_responded")
        self.added = b.sem("s5i_added")
        self.k_kept = b.sem("s5i_k_kept")
        self.x_kept = b.sem("s5i_x_kept")
        self.k_stored = [b.sem("s5i_k_even"), b.sem("s5i_k_odd")]
        self.cleared = b.sem("s5i_cleared")
        self.done = (self.x_kept, NB)

    def gpsimd(self, pool):
        b, m = self.b, self.m
        for s, v in self.sent:
            pool.wait_ge(s, v)
        for k in range(S5_C):
            pool.dma_start(m.u[16 * (7 - k):16 * (7 - k) + 16],
                           b.d_u.rearrange("(g h) t -> h g t", h=S5_H)[:, :, S5_J * k:S5_J * (k + 1)]
                           ).then_inc(self.u_in, 16)
        for s, v in self.needs:
            pool.wait_ge(s, v)

        def load(m_, par):
            pool.dma_start(m.ca[par], b.d_ca[m_]).then_inc(self.block_in[par], 16)
            pool.dma_start(m.pb[par], b.d_pb[m_]).then_inc(self.block_in[par], 16)

        def store(m_, par, n):
            pool.wait_ge(self.k_kept, n)
            pool.dma_start(b.d_k[m_], m.kpad[par]).then_inc(self.k_stored[par], 16)

        load(0, 0)
        load(1, 1)
        with pool.Fori(0, NB // 2 - 1) as it:
            for par in range(2):
                store(it * 2 + par, par, it * 2 + par + 1)
                pool.wait_ge(self.added, it * 2 + par + 1)
                load(it * 2 + par + 2, par)
        for par in range(2):
            store(NB - 2 + par, par, NB - 1 + par)

    def tensor(self, pe):
        b, m, mm = self.b, self.m, self.b.nc.tensor.matmul
        for s, v in self.needs:
            pe.wait_ge(s, v)
        pe.wait_ge(self.u_in, 16 * S5_C)

        def block(it, par):
            m_ = it * 2 + par
            pe.wait_ge(self.block_in[par], it * 32 + 32)
            if not isinstance(it, int) or it > 0:
                pe.wait_ge(self.k_kept, m_ - 1)
            for g in range(8):
                ins = mm(b.ps[0:S5_H, 2 * par + g // 4, g % 4 * P:(g % 4 + 1) * P], m.ca[par][:, g, 144:160],
                         m.ca[par][:, g, 0:P], start=True, stop=True)
            ins.then_inc(self.responded, 1)
            if not isinstance(it, int) or it > 0:
                pe.wait_ge(self.x_kept, m_ - 1)
            for g in range(8):
                ins = mm(b.ps[:, 4 + par, g * S5_J:(g + 1) * S5_J], m.pb[par][:, g, :], m.u[:, m_ * 8 + g, :],
                         start=True, stop=True)
            ins.then_inc(self.added, 1)

        self.loop(pe, block)

    def loop(self, eng, block):
        block(0, 0)
        block(0, 1)
        with eng.Fori(1, NB // 2) as it:
            for par in range(2):
                block(it, par)

    def scalar(self, act):
        b, m = self.b, self.m
        act.wait_ge(self.cleared, 3)

        def block(it, par):
            m_ = it * 2 + par
            act.wait_ge(self.responded, m_ + 1)
            if not isinstance(it, int) or it > 0:
                act.wait_ge(self.k_stored[par], it * 16)
            b.nc.scalar.activation(m.kpad[par][:, :, 112:240],
                                   b.ps[0:S5_H, 2 * par:2 * par + 2, :].rearrange("p b (g n) -> p (b g) n", g=4),
                                   ACT.Copy).then_inc(self.k_kept, 1)
        self.loop(act, block)

    def vector(self, dve):
        b, m, v = self.b, self.m, self.b.nc.vector
        for s, n in self.needs:
            dve.wait_ge(s, n)
        v.memset(m.kpad[0][:, :, 0:112], 0.0).then_inc(self.cleared, 1)
        v.memset(m.kpad[1][:, :, 0:112], 0.0).then_inc(self.cleared, 1)
        v.memset(m.state[:, 0, :], 0.0).then_inc(self.cleared, 1)

        def block(it, par):
            m_ = it * 2 + par
            dve.wait_ge(self.added, m_ + 1)
            to = m.state[:, 1:S5_J + 1, bass.ds(m_ * 8, 8)].rearrange("p j g -> p g j")
            v.tensor_copy(to, b.ps[:, 4 + par, :].rearrange("p (g j) -> p g j", g=8)).then_inc(self.x_kept, 1)
        self.loop(dve, block)


class S5Scan(Stage):

    def __init__(self, b, m, needs):
        self.b, self.m, self.needs = b, m, needs
        self.step = b.sem("s5s_step")
        self.done = (self.step, 5 * S5_J)

    def vector(self, dve):
        b, m, tt = self.b, self.m, self.b.nc.vector.tensor_tensor
        for s, n in self.needs:
            dve.wait_ge(s, n)
        lo, hi = slice(0, S5_P), slice(S5_P, P)
        with dve.Fori(0, S5_J) as j:
            old, new = m.state[:, j, :], m.state[:, j + 1, :]
            tt(m.t1, b.a8[:, 0, :], old, ALU.mult).then_inc(self.step, 1)
            tt(m.t2[lo], b.a8[hi, 1, :], old[hi], ALU.mult).then_inc(self.step, 1)
            tt(m.t2[hi], b.a8[lo, 1, :], old[lo], ALU.mult).then_inc(self.step, 1)
            dve.wait_ge(self.step, j * 5 + 1)
            tt(new, new, m.t1, ALU.add).then_inc(self.step, 1)
            dve.wait_ge(self.step, j * 5 + 4)
            tt(new, new, m.t2, ALU.add).then_inc(self.step, 1)
            dve.wait_ge(self.step, j * 5 + 5)

    def tensor(self, pe):
        pass

    def scalar(self, act):
        pass


class S5Outputs(Stage):

    def __init__(self, b, m, needs):
        self.b, self.m, self.needs = b, m, needs
        self.block_in = [b.sem("s5o_in_even"), b.sem("s5o_in_odd")]
        self.mixed = b.sem("s5o_mixed")
        self.kept = b.sem("s5o_kept")
        self.sent = [b.sem("s5o_sent_even"), b.sem("s5o_sent_odd")]
        self.back = [b.sem("s5o_back_even"), b.sem("s5o_back_odd")]
        self.skipped = b.sem("s5o_skipped")
        self.gelued = b.sem("s5o_gelued")
        self.done = (self.gelued, NB)

    loop = S5Inputs.loop

    def gpsimd(self, pool):
        b, m = self.b, self.m
        for s, v in self.needs:
            pool.wait_ge(s, v)

        def load(m_, par):
            pool.dma_start(m.ca[par], b.d_ca[m_]).then_inc(self.block_in[par], 16)
            for k in range(S5_C):
                pool.dma_start(m.toep[par][16 * k:16 * k + 16], b.d_k[m_][:, :, 16 * k:16 * k + P]
                               ).then_inc(self.block_in[par], 16)

        def fetch(m_, par, n):
            pool.wait_ge(self.sent[par], n)
            pool.dma_start(m.y[:, m_, :], b.d_y.rearrange("(m p) t -> m p t", p=P)[m_]).then_inc(self.back[par], 16)
            pool.dma_start(m.ustage[par], b.d_u.rearrange("(m p) t -> m p t", p=P)[m_]).then_inc(self.back[par], 16)

        def turn(it, par):
            m_ = it * 2 + par
            if not isinstance(it, int) or it > 1:
                pool.wait_ge(self.skipped, m_ - 3)
            if not isinstance(it, int) or it > 0:
                fetch(m_ - 2, par, it * (16 * S5_C))

        def load_next(it, par):
            pool.wait_ge(self.mixed, it * 2 + par + 1)
            load(it * 2 + par + 2, par)

        load(0, 0)
        load(1, 1)
        for it in range(2):
            for par in range(2):
                turn(it, par)
                load_next(it, par)
        with pool.Fori(2, NB // 2 - 1) as it:
            for par in range(2):
                turn(it, par)
                load_next(it, par)
        for par in range(2):
            turn(NB // 2 - 1, par)
        for m_ in (NB - 2, NB - 1):
            pool.wait_ge(self.skipped, m_ - 1)
            fetch(m_, m_ % 2, (m_ // 2 + 1) * 16 * S5_C)

    def tensor(self, pe):
        b, m, mm = self.b, self.m, self.b.nc.tensor.matmul
        for s, v in self.needs:
            pe.wait_ge(s, v)

        def block(it, par):
            m_ = it * 2 + par
            pe.wait_ge(self.block_in[par], it * (16 * 9) + 16 * 9)
            if not isinstance(it, int) or it > 0:
                pe.wait_ge(self.kept, m_ - 1)
            for g in range(8):
                to = b.ps[:, par, g * S5_J:(g + 1) * S5_J]
                mm(to, m.toep[par][:, g, :], m.u[:, m_ * 8 + g, :], start=True, stop=False)
                ins = mm(to, m.ca[par][:, g, 16:144], m.state[:, 0:S5_J, m_ * 8 + g], start=False, stop=True)
            ins.then_inc(self.mixed, 1)
        self.loop(pe, block)

    def scalar(self, act):
        b, m, f = self.b, self.m, self.b.nc.scalar.activation
        for s, n in self.needs:
            act.wait_ge(s, n)

        def block(it, par):
            m_ = it * 2 + par
            act.wait_ge(self.mixed, m_ + 1)
            if not isinstance(it, int) or it > 0:
                act.wait_ge(self.sent[par], it * (16 * S5_C))
            f(m.ystage[par], b.ps[:, par, :].rearrange("p (g j) -> p g j", g=8), ACT.Copy).then_inc(self.kept, 1)
            act.wait_ge(self.kept, m_ + 1)
            for i in range(S5_C):
                act.dma_start(b.d_y.rearrange("(m g h) t -> m h g t", g=8, h=S5_H)[m_][:, :, S5_J * i:S5_J * (i + 1)],
                              m.ystage[par][16 * i:16 * i + 16]).then_inc(self.sent[par], 16)

        def gelu(m_):
            act.wait_ge(self.skipped, m_ + 1)
            f(m.y[:, m_, :], m.y[:, m_, :], ACT.Gelu_apprx_tanh).then_inc(self.gelued, 1)

        self.loop(act, block)
        with act.Fori(0, NB) as i:
            gelu(i)

    def vector(self, dve):
        b, m = self.b, self.m

        def skip(m_, par, n):
            dve.wait_ge(self.back[par], n)
            y = m.y[:, m_, :]
            b.nc.vector.scalar_tensor_tensor(out=y, in0=m.ustage[par], scalar=b.cols[:, bass.ds(m_ + col_at("s5_d"), 1)],
                                             in1=y, op0=ALU.mult, op1=ALU.add).then_inc(self.skipped, 1)
        with dve.Fori(0, NB // 2) as it:
            for par in range(2):
                skip(it * 2 + par, par, it * 32 + 32)


RW_PAIRS = 4
RW_N = 64
RW_C = 32
TOK_TILES = [(t * P, min(P, L2 - t * P)) for t in range(-(-L2 // P))]
N_CHUNKS = -(-L2 // RW_C)
RANGES2 = HALVES


class Shift(Stage):

    def __init__(self, b, y, diff, tiles):
        self.b, self.y, self.diff, self.tiles = b, y, diff, tiles
        self.shifted = b.sem("shifted")

    def vector(self, dve):
        b, v, d = self.b, self.b.nc.vector, self.diff
        link = b.chain.link
        for n, (m, full) in enumerate(self.tiles):
            y = self.y(m)
            dve.wait_ge(*full)
            v.tensor_scalar(d[:, 0:1], y[:, 0:1], -1.0, None, ALU.mult)
            link(v.tensor_tensor(d[:, 1:L2], y[:, 0:L2 - 1], y[:, 1:L2], ALU.subtract))
            v.scalar_tensor_tensor(out=y, in0=d, scalar=self.b.col("ev_mu_2", m), in1=y,
                                   op0=ALU.mult, op1=ALU.add).then_inc(self.shifted, 1)
            dve.wait_ge(self.shifted, n + 1)


class RwkvPrepare(Stage):

    def __init__(self, b, m, needs):
        self.b, self.m, self.needs = b, m, needs
        self.started = b.sem("rwp_started")
        self.products = b.sem("rwp_products")
        self.rooted = b.sem("rwp_rooted")
        self.exped = b.sem("rwp_exped")
        self.copied = b.sem("rwp_copied")
        self.squared = b.sem("rwp_squared")
        self.bonus_in = b.sem("rwp_bonus_in")
        self.bonused = b.sem("rwp_bonused")
        self.arg = b.sem("rwp_arg")
        self.norm_in = b.sem("rwp_norm_in")
        self.prepared = b.sem("rwp_prepared")
        self.done = (self.prepared, RW_PAIRS)

    def tensor(self, pe):
        b, m, mm = self.b, self.m, self.b.nc.tensor.matmul
        pe.wait_ge(self.started, 2)
        for j in range(RW_PAIRS):
            cols = slice(j * P, (j + 1) * P)
            if j:
                pe.wait_ge(self.copied, 3 * j)
                pe.wait_ge(self.bonused, j)
            lo, hi = slice(0, RW_N), slice(RW_N, P)
            for bank, w, x in ((0, m.w_wa[lo, cols], m.y(12)[lo]), (2, m.w_wa[hi, cols], m.y(12)[hi]),
                               (4, m.w_g[:, cols], m.y(13))):
                for i, (t0, tn) in enumerate(RANGES2):
                    ins = mm(b.ps[:, bank + i, 0:tn], w, x[:, t0:t0 + tn], start=True, stop=True)
                ins.then_inc(self.products, 1)
            pe.wait_ge(self.squared, j + 1)
            if j:
                pe.wait_ge(self.rooted, 2 * j)
            for i, (t0, tn) in enumerate(RANGES2):
                ins = mm(b.ps[:, 6 + i, 0:tn], b.ones64, m.t_sq[:, t0:t0 + tn], start=True, stop=True)
            ins.then_inc(self.norm_in, 1)
            pe.wait_ge(self.bonus_in, j + 1)
            for i, (t0, tn) in enumerate(RANGES2):
                ins = mm(b.ps[:, i, 0:tn], b.ones64, m.t_bonus[:, t0:t0 + tn], start=True, stop=True)
            ins.then_inc(self.products, 1)

    def scalar(self, act):
        b, m, f = self.b, self.m, self.b.nc.scalar.activation
        for s, n in self.needs:
            act.wait_ge(s, n)
        lo = slice(0, RW_N)
        f(m.y(12)[lo], m.y(12)[lo], ACT.Tanh).then_inc(self.started, 1)
        f(m.y(13), m.y(13), ACT.Sigmoid).then_inc(self.started, 1)
        both = lambda bank: b.ps[:, bank:bank + 2, 0:L2 // 2]
        two = lambda ap: ap.rearrange("p (r t) -> p r t", r=2)
        for j in range(RW_PAIRS):
            if j:
                act.wait_ge(self.prepared, j)
            f(m.t_sq, m.y(4 + j), ACT.Square, scale=b.col("ev_k_k_2", j)).then_inc(self.squared, 1)
            act.wait_ge(self.products, 4 * j + 1)
            f(two(m.t_w), both(0), ACT.Sigmoid, bias=b.col("ev_w0_2", j)).then_inc(self.copied, 1)
            act.wait_ge(self.products, 4 * j + 2)
            f(two(m.t_a), both(2), ACT.Sigmoid, bias=b.col("ev_a0_2", j)).then_inc(self.copied, 1)
            act.wait_ge(self.products, 4 * j + 3)
            f(two(m.g(j)), both(4), ACT.Copy).then_inc(self.copied, 1)
            act.wait_ge(self.norm_in, j + 1)
            for i, (t0, tn) in enumerate(RANGES2):
                f(m.t_norm[:, t0:t0 + tn], b.ps[:, 6 + i, 0:tn], ACT.Sqrt).then_inc(self.rooted, 1)
            act.wait_ge(self.arg, j + 1)
            f(m.t_pos, m.t_cum, ACT.Exp).then_inc(self.exped, 1)
            f(m.t_neg, m.t_cum, ACT.Exp, scale=-1.0).then_inc(self.exped, 1)
            f(m.t_before, m.t_w, ACT.Exp).then_inc(self.exped, 1)

    def vector(self, dve):
        b, m, v = self.b, self.m, self.b.nc.vector
        tt, ts, stt = v.tensor_tensor, v.tensor_scalar, v.scalar_tensor_tensor
        link = b.chain.link
        for s, n in self.needs:
            dve.wait_ge(s, n)
        at = col_at("ev_k_a_2")
        link(ts(m.rest_a, b.cols[:, at:at + 4], -1.0, 1.0, ALU.mult, ALU.add))
        for j in range(RW_PAIRS):
            r, k, val = m.y(j), m.y(4 + j), m.y(8 + j)
            dve.wait_ge(self.copied, 3 * j + 1)
            link(ts(m.t_w, m.t_w, -float(np.exp(-0.5)), None, ALU.mult))
            link(v.tensor_tensor_scan(m.t_cum, b.restart32, m.t_w, 0.0, ALU.mult, ALU.add))
            tt(m.t_w, m.t_cum, m.t_w, ALU.subtract).then_inc(self.arg, 1)
            dve.wait_ge(self.copied, 3 * j + 2)
            link(ts(m.t_k, m.t_a, b.col("ev_k_a_2", j), m.rest_a[:, j:j + 1], ALU.mult, ALU.add))
            link(tt(m.t_k, m.t_k, k, ALU.mult))
            stt(out=m.t_bonus, in0=r, scalar=b.col("ev_r_k_2", j), in1=m.t_k, op0=ALU.mult,
                op1=ALU.mult).then_inc(self.bonus_in, 1)
            dve.wait_ge(self.rooted, 2 * j + 2)
            link(ts(m.t_norm, m.t_norm, 1e-12, None, ALU.max))
            link(v.reciprocal(m.t_norm, m.t_norm))
            link(stt(out=m.t_norm, in0=k, scalar=b.col("ev_k_k_2", j), in1=m.t_norm, op0=ALU.mult, op1=ALU.mult))
            link(tt(m.t_a, m.t_a, m.t_norm, ALU.mult))
            dve.wait_ge(self.exped, 3 * j + 3)
            tt(r, r, m.t_pos, ALU.mult)
            tt(k, m.t_k, m.t_neg, ALU.mult)
            tt(m.be(j), m.t_a, m.t_neg, ALU.mult)
            stt(out=m.al(j), in0=m.t_norm, scalar=-1.0, in1=m.t_before, op0=ALU.mult, op1=ALU.mult)
            v.tensor_copy(m.end[:, j, 0:16], m.t_pos[:, 0:512].rearrange("p (c t) -> p c t", t=RW_C)[:, :, RW_C - 1])
            v.tensor_copy(m.end[:, j, 16:17], m.t_pos[:, L2 - 1:L2])
            dve.wait_ge(self.products, 4 * j + 4)
            tt(m.bonus(j).rearrange("p (r t) -> p r t", r=2), b.ps[:, 0:2, 0:L2 // 2],
               val.rearrange("p (r t) -> p r t", r=2), ALU.mult).then_inc(self.bonused, 1)
            dve.wait_ge(self.bonused, j + 1)
            v.tensor_copy(m.one, m.one2).then_inc(self.prepared, 1)


class Rwkv(Stage):

    def __init__(self, b, m, needs, pool):
        self.b, self.m, self.needs, self.pool = b, m, needs, pool
        self.grams = b.sem("rw_grams")
        self.turned = b.sem("rw_turned")
        self.masked = b.sem("rw_masked")
        self.mk_masked = b.sem("rw_mk_masked")
        self.toks = b.sem("rw_toks")
        self.squares = b.sem("rw_squares")
        self.zsq = b.sem("rw_zsq")
        self.ysq = b.sem("rw_ysq")
        self.invp = b.sem("rw_invp")
        self.inv = b.sem("rw_inv")
        self.u_in = b.sem("rw_u_in")
        self.u_kept = b.sem("rw_u_kept")
        self.p_in = b.sem("rw_p_in")
        self.p_kept = b.sem("rw_p_kept")
        self.r_in = b.sem("rw_r_in")
        self.r_kept = b.sem("rw_r_kept")
        self.oc_in = b.sem("rw_oc_in")
        self.oc_kept = b.sem("rw_oc_kept")
        self.ab_in = b.sem("rw_ab_in")
        self.a_masked = b.sem("rw_a_masked")
        self.a_kept = b.sem("rw_a_kept")
        self.b_kept = b.sem("rw_b_kept")
        self.s_in = b.sem("rw_s_in")
        self.s_kept = b.sem("rw_s_kept")
        self.o_in = b.sem("rw_o_in")
        self.o_kept = b.sem("rw_o_kept")
        self.cleared = b.sem("rw_cleared")
        self.groups = 2 * len(TOK_TILES)
        self.done = [(self.o_kept, N_CHUNKS)]

    def chunks(self, tau):
        return -(-TOK_TILES[tau][1] // RW_C)

    def tensor(self, pe):
        b, m, mm = self.b, self.m, self.b.nc.tensor.matmul
        for s, n in self.needs:
            pe.wait_ge(s, n)

        def chain(tau, c):
            t0, nt = TOK_TILES[tau]
            i = 4 * tau + c
            c0, cn = t0 + RW_C * c, min(RW_C, nt - RW_C * c)
            if c == 0:
                for sem in (self.b_kept, self.a_kept, self.r_kept, self.oc_kept):
                    pe.wait_ge(sem, 2 * tau + 2)
            if i:
                pe.wait_ge(self.s_kept, 4 * i)
                pe.wait_ge(self.o_kept, i)
            else:
                pe.wait_ge(self.cleared, 1)
            for j in range(RW_PAIRS):
                ins = mm(b.ps[:, 7, j * RW_C:j * RW_C + cn], m.s[:, i % 2, j, :], m.y(j)[:, c0:c0 + cn],
                         start=True, stop=True)
            ins.then_inc(self.o_in, 1)
            for j in range(RW_PAIRS):
                ins = mm(b.ps[:, 5 + i % 2, j * P:(j + 1) * P], m.a[:, j, c, :], m.s[:, i % 2, j, :], start=True, stop=True)
            ins.then_inc(self.s_in, 1)

        for n in range(self.groups):
            tau, half = divmod(n, 2)
            t0, nt = TOK_TILES[tau]
            tok, T = slice(t0, t0 + nt), slice(0, nt)
            nch = self.chunks(tau)
            if n:
                pe.wait_ge(self.b_kept, n)
                pe.wait_ge(self.a_masked, n)
                pe.wait_ge(self.r_kept, n)
                pe.wait_ge(self.oc_kept, n)
            for q in range(4):
                j, rows = 2 * half + q // 2, slice(RW_N * (q % 2), RW_N * (q % 2) + RW_N)
                al, be, k, r = (x[rows, tok] for x in (m.al(j), m.be(j), m.y(4 + j), m.y(j)))
                for i, (lhs, rhs) in enumerate(((al, be), (be, al), (k, al), (be, r))):
                    ins = mm(b.ps[T, q, i * P:i * P + nt], lhs, rhs, start=True, stop=True)
                ins.then_inc(self.grams, 1)
            for odd in range(2):
                rows = slice(RW_N * odd, RW_N * odd + RW_N)
                for p in range(2):
                    j = 2 * half + p
                    ins = mm(b.ps[T, 4 + 3 * odd, p * P:p * P + nt], m.y(4 + j)[rows, tok], m.y(j)[rows, tok],
                             start=True, stop=True)
                ins.then_inc(self.grams, 1)
            for p in range(2):
                j = 2 * half + p
                for i, x in enumerate((m.al(j), m.be(j), m.y(4 + j), m.y(8 + j))):
                    ins = b.nc.tensor.transpose(b.ps[T, 5 + p, i * P:(i + 1) * P], x[:, tok], b.ident[:, :])
                ins.then_inc(self.turned, 1)
            pe.wait_ge(self.masked, 4 * n + 4)
            for lvl in range(4):
                if lvl == 0:
                    y = lambda q: m.gram[T, q, 0, 0:nt]
                    z = lambda q: m.gram[T, q, 1, 0:nt]
                else:
                    y = lambda q, l=lvl: m.pw[T, (l - 1) % 2, 0, q, 0:nt]
                    z = lambda q, l=lvl: m.pw[T, (l - 1) % 2, 1, q, 0:nt]
                    pe.wait_ge(self.ysq, 4 * n + lvl)
                    if lvl < 4:
                        pe.wait_ge(self.zsq, 3 * n + min(lvl, 3))
                for q in range(4):
                    ins = mm(b.ps[T, 0, q * P:q * P + nt], z(q), y(q), start=True, stop=True)
                ins.then_inc(self.squares, 1)
                if lvl < 3:
                    for q in range(4):
                        ins = mm(b.ps[T, 1, q * P:q * P + nt], y(q), z(q), start=True, stop=True)
                    ins.then_inc(self.squares, 1)
                if half == 0 and tau:
                    if lvl == 0:
                        pe.wait_ge(self.mk_masked, 2 * n + 2)
                        pe.wait_ge(self.toks, 4 * n + 4)
                    chain(tau - 1, lvl)
                pe.wait_ge(self.ysq, 4 * n + lvl + 1)
                pe.wait_ge(self.inv, 5 * n + lvl + 1)
                for q in range(4):
                    ins = mm(b.ps[T, 2, q * P:q * P + nt], m.pw[T, lvl % 2, 0, q, 0:nt], m.inv[T, q, 0:nt],
                             start=True, stop=True)
                ins.then_inc(self.invp, 1)
            pe.wait_ge(self.toks, 4 * n + 4)
            for q in range(4):
                ins = mm(b.ps[T, 3, q * RW_N:(q + 1) * RW_N], m.gram[T, q, 2, 0:nt],
                         m.bkv[T, q // 2, 2, (q % 2) * RW_N:(q % 2 + 1) * RW_N], start=True, stop=True)
            ins.then_inc(self.u_in, 1)
            pe.wait_ge(self.u_kept, n + 1)
            pe.wait_ge(self.inv, 5 * n + 5)
            pe.wait_ge(self.mk_masked, 2 * n + 2)
            for q in range(4):
                ins = mm(b.ps[T, 4, q * P:(q + 1) * P], m.inv[T, q, 0:nt], m.au[T, q, :], start=True, stop=True)
            ins.then_inc(self.p_in, 1)
            pe.wait_ge(self.p_kept, n + 1)
            if half == 0 and tau:
                pe.wait_ge(self.s_kept, 16 * tau)
                pe.wait_ge(self.o_kept, 4 * tau)
            for q in range(4):
                rows = slice(RW_N * (q % 2), RW_N * (q % 2) + RW_N)
                ins = mm(b.ps[rows, 5, (q // 2) * P:(q // 2) * P + nt], m.p[T, 0, q, :], m.gram[T, q, 3, 0:nt],
                         start=True, stop=True)
            ins.then_inc(self.r_in, 1)
            for q in range(4):
                rows = slice(RW_N * (q % 2), RW_N * (q % 2) + RW_N)
                o = b.ps[rows, 6, (q // 2) * P:(q // 2) * P + nt]
                mm(o, m.p[T, 1, q, :], m.gram[T, q, 3, 0:nt], start=True, stop=False)
                ins = mm(o, m.bkv[T, q // 2, 2, (q % 2) * RW_N:(q % 2 + 1) * RW_N], m.mk[T, q, 0:nt],
                         start=False, stop=True)
            ins.then_inc(self.oc_in, 1)
            for c in range(nch):
                rows = slice(RW_C * c, min(RW_C * c + RW_C, nt))
                for p in range(2):
                    ins = mm(b.ps[:, c, p * P:(p + 1) * P], m.p[rows, 0, 2 * p:2 * p + 2, :].rearrange("t h k -> t (h k)"), m.bkv[rows, p, 0, :],
                             start=True, stop=True)
                for p in range(2):
                    o = b.ps[:, c, (2 + p) * P:(3 + p) * P]
                    mm(o, m.bkv[rows, p, 0, :], m.p[rows, 1, 2 * p:2 * p + 2, :].rearrange("t h k -> t (h k)"), start=True, stop=False)
                    ins = mm(o, m.bkv[rows, p, 1, :], m.bkv[rows, p, 2, :], start=False, stop=True)
            ins.then_inc(self.ab_in, 1)
        chain(self.groups // 2 - 1, 0)

    def scalar(self, act):
        b, m, f = self.b, self.m, self.b.nc.scalar.activation
        for n in range(self.groups):
            tau, half = divmod(n, 2)
            t0, nt = TOK_TILES[tau]
            T = slice(0, nt)
            for p in range(2):
                act.wait_ge(self.turned, 2 * n + p + 1)
                if n:
                    act.wait_ge(self.ab_in, n)
                ps = b.ps[T, 5 + p, :]
                f(m.au[T, 2 * p:2 * p + 2, 0:RW_N], ps[:, 0:P].rearrange("p (h k) -> p h k", h=2), ACT.Copy
                  ).then_inc(self.toks, 1)
                f(m.bkv[T, p], ps[:, P:4 * P].rearrange("p (i k) -> p i k", i=3), ACT.Copy).then_inc(self.toks, 1)
            for lvl in range(4):
                act.wait_ge(self.squares, 7 * n + 2 * lvl + 1)
                if lvl >= 2:
                    act.wait_ge(self.invp, 4 * n + lvl - 1)
                f(m.pw[T, lvl % 2, 0, :, 0:nt], b.ps[T, 0, :].rearrange("p (q s) -> p q s", q=4)[:, :, 0:nt],
                  ACT.Copy).then_inc(self.ysq, 1)
            act.wait_ge(self.u_in, n + 1)
            f(m.au[T, :, RW_N:P], b.ps[T, 3, 0:4 * RW_N].rearrange("p (q v) -> p q v", q=4), ACT.Copy).then_inc(self.u_kept, 1)
            act.wait_ge(self.p_in, n + 1)
            f(m.p[T].rearrange("t s q k -> t q s k"), b.ps[T, 4, :].rearrange("p (q s k) -> p q s k", q=4, s=2), ACT.Copy).then_inc(self.p_kept, 1)
            act.wait_ge(self.oc_in, n + 1)
            f(m.o4[:, 2 * half:2 * half + 2, t0:t0 + nt], b.ps[:, 6, 0:2 * P].rearrange("p (q t) -> p q t", q=2)[:, :, 0:nt],
              ACT.Copy).then_inc(self.oc_kept, 1)

    def vector(self, dve):
        b, m, v = self.b, self.m, self.b.nc.vector
        tt, ts, stt = v.tensor_tensor, v.tensor_scalar, v.scalar_tensor_tensor
        for s, n in self.needs:
            dve.wait_ge(s, n)
        v.memset(m.s[:, 0], 0.0).then_inc(self.cleared, 1)

        def chain(tau, c):
            t0, nt = TOK_TILES[tau]
            i, cn = 4 * tau + c, min(RW_C, nt - RW_C * c)
            if c == 0:
                dve.wait_ge(self.b_kept, 2 * tau + 2)
                dve.wait_ge(self.oc_kept, 2 * tau + 2)
            dve.wait_ge(self.s_in, i + 1)
            for j in range(RW_PAIRS):
                stt(out=m.s[:, (i + 1) % 2, j, :], in0=b.ps[:, 5 + i % 2, j * P:(j + 1) * P],
                    scalar=m.end[:, j, i:i + 1], in1=m.bb[:, j, c, :],
                    op0=ALU.mult, op1=ALU.add).then_inc(self.s_kept, 1)
            o = m.o4[:, :, t0 + RW_C * c:t0 + RW_C * c + cn]
            tt(o, o, b.ps[:, 7, 0:4 * RW_C].rearrange("p (j t) -> p j t", j=4)[:, :, 0:cn], ALU.add).then_inc(self.o_kept, 1)

        for n in range(self.groups):
            tau, half = divmod(n, 2)
            t0, nt = TOK_TILES[tau]
            T = slice(0, nt)
            nch = self.chunks(tau)
            four = lambda bank: b.ps[T, bank, :].rearrange("p (q s) -> p q s", q=4)[:, :, 0:nt]
            for q in range(4):
                dve.wait_ge(self.grams, 6 * n + q + 1)
                tt(m.gram[T, q, :, 0:nt], four(q), b.masks[T, :, 0:nt], ALU.mult).then_inc(self.masked, 1)
            dve.wait_ge(self.masked, 4 * n + 4)
            tt(m.inv[T, :, 0:nt], m.gram[T, :, 1, 0:nt], b.ident[T, 0:nt].unsqueeze(1).broadcast_to([nt, 4, nt]),
               ALU.add).then_inc(self.inv, 1)
            for odd in range(2):
                dve.wait_ge(self.grams, 6 * n + 5 + odd)
                tt(m.mk[T, odd:4:2, 0:nt], b.ps[T, 4 + 3 * odd, 0:2 * P].rearrange("p (q s) -> p q s", q=2)[:, :, 0:nt],
                   b.masks[T, 3, 0:nt].unsqueeze(1).broadcast_to([nt, 2, nt]), ALU.mult).then_inc(self.mk_masked, 1)
            for lvl in range(4):
                if lvl < 3:
                    dve.wait_ge(self.squares, 7 * n + 2 * lvl + 2)
                    v.tensor_copy(m.pw[T, lvl % 2, 1, :, 0:nt], four(1)).then_inc(self.zsq, 1)
                if half == 0 and tau:
                    chain(tau - 1, lvl)
                dve.wait_ge(self.invp, 4 * n + lvl + 1)
                dve.wait_ge(self.inv, 5 * n + lvl + 1)
                tt(m.inv[T, :, 0:nt], m.inv[T, :, 0:nt], four(2), ALU.add).then_inc(self.inv, 1)
            if n < 4:
                self.pool.vector_tile(dve, n)
            dve.wait_ge(self.r_in, n + 1)
            if half == 0 and tau:
                dve.wait_ge(self.s_kept, 16 * tau)
                dve.wait_ge(self.o_kept, 4 * tau)
            y4 = m.y4[:, 2 * half:2 * half + 2, t0:t0 + nt]
            tt(y4, y4, b.ps[:, 5, 0:2 * P].rearrange("p (q t) -> p q t", q=2)[:, :, 0:nt], ALU.add).then_inc(self.r_kept, 1)
            dve.wait_ge(self.ab_in, n + 1)
            tt(m.a[:, 2 * half:2 * half + 2, 0:nch, :],
               b.ps[:, 0:nch, 0:2 * P].rearrange("p c (q k) -> p q c k", k=P),
               b.same64.unsqueeze(1).unsqueeze(1).broadcast_to([P, 2, nch, P]), ALU.mult).then_inc(self.a_masked, 1)
            for p in range(2):
                for c in range(nch):
                    ins = stt(out=m.bb[:, 2 * half + p, c, :], in0=b.ps[:, c, (2 + p) * P:(3 + p) * P],
                              scalar=m.end[:, 2 * half + p, 4 * tau + c:4 * tau + c + 1], in1=b.same64,
                              op0=ALU.mult, op1=ALU.mult)
            ins.then_inc(self.b_kept, 1)
        chain(self.groups // 2 - 1, 0)
        dve.wait_ge(self.s_kept, 4 * N_CHUNKS)
        dve.wait_ge(self.o_kept, N_CHUNKS)

    def gpsimd(self, pool):
        b, m = self.b, self.m
        for n in range(self.groups):
            half, nch = n % 2, self.chunks(n // 2)
            pool.wait_ge(self.a_masked, n + 1)
            a = m.a[:, 2 * half:2 * half + 2, 0:nch, :]
            b.nc.gpsimd.tensor_tensor(a, a, b.ident[:, :].unsqueeze(1).unsqueeze(1).broadcast_to([P, 2, nch, P]),
                                      ALU.add).then_inc(self.a_kept, 1)


class RwkvFinish(Stage):

    def __init__(self, b, m, needs, pool):
        self.b, self.m, self.needs, self.pool = b, m, needs, pool
        self.mean_in = b.sem("rwf_mean_in")
        self.centred = b.sem("rwf_centred")
        self.squared = b.sem("rwf_squared")
        self.var_in = b.sem("rwf_var_in")
        self.rooted = b.sem("rwf_rooted")
        self.finished = b.sem("rwf_finished")
        self.done = (self.finished, RW_PAIRS)

    def tensor(self, pe):
        b, m, mm = self.b, self.m, self.b.nc.tensor.matmul
        for s, n in self.needs:
            pe.wait_ge(s, n)

        def mean(j):
            if j:
                pe.wait_ge(self.centred, j)
            for i, (t0, tn) in enumerate(RANGES2):
                ins = mm(b.ps[:, i, 0:tn], b.ones64, m.o4[:, j, t0:t0 + tn], start=True, stop=True)
            ins.then_inc(self.mean_in, 1)

        mean(0)
        for j in range(RW_PAIRS):
            if j + 1 < RW_PAIRS:
                mean(j + 1)
            self.pool.tensor_tile(pe, j)
            pe.wait_ge(self.squared, j + 1)
            if j:
                pe.wait_ge(self.rooted, 2 * j)
            for i, (t0, tn) in enumerate(RANGES2):
                ins = mm(b.ps[:, 2 + i, 0:tn], b.ones64, m.t_sq[:, t0:t0 + tn], start=True, stop=True)
            ins.then_inc(self.var_in, 1)

    def scalar(self, act):
        b, m, f = self.b, self.m, self.b.nc.scalar.activation
        for j in range(RW_PAIRS):
            act.wait_ge(self.centred, j + 1)
            if j:
                act.wait_ge(self.var_in, j)
            f(m.t_sq, m.o4[:, j, :], ACT.Square).then_inc(self.squared, 1)
            act.wait_ge(self.var_in, j + 1)
            if j:
                act.wait_ge(self.finished, j)
            for i, (t0, tn) in enumerate(RANGES2):
                f(m.t_norm[:, t0:t0 + tn], b.ps[:, 2 + i, 0:tn], ACT.Sqrt, scale=1 / RW_N,
                  bias=b.eps[64 * 1e-5]).then_inc(self.rooted, 1)
            self.pool.scalar_tile(act, j)

    def vector(self, dve):
        b, m, v = self.b, self.m, self.b.nc.vector
        tt, ts, stt = v.tensor_tensor, v.tensor_scalar, v.scalar_tensor_tensor
        link = b.chain.link
        two = lambda ap: ap.rearrange("p (r t) -> p r t", r=2)

        def centre(j):
            o = two(m.o4[:, j, :])
            dve.wait_ge(self.mean_in, j + 1)
            stt(out=o, in0=b.ps[:, 0:2, 0:L2 // 2], scalar=-1 / RW_N, in1=o, op0=ALU.mult,
                op1=ALU.add).then_inc(self.centred, 1)

        centre(0)
        for j in range(RW_PAIRS):
            if j + 1 < RW_PAIRS:
                centre(j + 1)
            o = m.o4[:, j, :]
            dve.wait_ge(self.rooted, 2 * j + 2)
            link(v.reciprocal(m.t_norm, m.t_norm))
            link(stt(out=o, in0=o, scalar=b.col("ev_ln_w_2", j), in1=m.t_norm, op0=ALU.mult, op1=ALU.mult))
            link(stt(out=o, in0=o, scalar=b.col("ev_ln_b_2", j), in1=m.bonus(j), op0=ALU.add, op1=ALU.add))
            tt(o, o, m.g(j), ALU.mult).then_inc(self.finished, 1)
            dve.wait_ge(self.finished, j + 1)


class Pool:

    def __init__(self, b, m, needs):
        self.b, self.m, self.needs = b, m, needs
        self.meaned = b.sem("pool_meaned")
        self.mixed, self.done_ = b.sem("pool_mixed"), b.sem("pool_done")
        self.done = (self.done_, 4)

    def vector_tile(self, dve, i):
        b, m, v = self.b, self.m, self.b.nc.vector
        link = b.chain.link
        if i == 0:
            for s, n in self.needs:
                dve.wait_ge(s, n)
        src, shift = m.y(14 + i), 1
        for lvl in range(i + 1):
            to = m.sums[lvl % 2]
            v.tensor_copy(to[:, 0:shift], src[:, 0:shift])
            link(v.tensor_tensor(to[:, shift:L2], src[:, shift:L2], src[:, 0:L2 - shift], ALU.add))
            src, shift = to, 2 * shift
        link(v.tensor_tensor(src[:, 0:16], src[:, 0:16], b.early[:, 16 * i:16 * i + 16], ALU.mult))
        u = m.y(14 + i)
        v.scalar_tensor_tensor(out=u, in0=src, scalar=1.0 / shift, in1=u, op0=ALU.mult,
                               op1=ALU.subtract).then_inc(self.meaned, 1)
        dve.wait_ge(self.meaned, i + 1)

    def tensor_tile(self, pe, i):
        b, m = self.b, self.m
        pe.wait_ge(self.meaned, i + 1)
        if i:
            pe.wait_ge(self.done_, i)
        for r, (t0, tn) in enumerate(RANGES2):
            ins = b.nc.tensor.matmul(b.ps[:, 4 + r, 0:tn], m.w_pool[:, i, :], m.y(14 + i)[:, t0:t0 + tn],
                                     start=True, stop=True)
        ins.then_inc(self.mixed, 1)

    def scalar_tile(self, act, i):
        b, m = self.b, self.m
        act.wait_ge(self.mixed, i + 1)
        b.nc.scalar.activation(m.y(14 + i).rearrange("p (r t) -> p r t", r=2), b.ps[:, 4:6, 0:L2 // 2],
                               ACT.Copy, scale=b.col("ev_pool_scale_2", i)).then_inc(self.done_, 1)


DIFF_HEADS = 8
DIFF_DIM = D // (2 * DIFF_HEADS)
LAM_INIT = 0.8 - 0.6 * float(np.exp(-0.3))


class SplitZ(Stage):

    def __init__(self, b, use, needs):
        self.b, self.needs, self.n = b, needs, MIX // P
        self.base = 2 * self.n * use
        self.ready = lambda k: (b.z_parts, self.base + min(2 * k + 3, 2 * self.n))

    def vector(self, dve):
        b, v = self.b, self.b.nc.vector
        for s, n in self.needs:
            dve.wait_ge(s, n)
        for k in range(self.n + 1):
            if k < self.n:
                v.tensor_copy(b.z_hi[:, k, :], b.z[:, k, :]).then_inc(b.z_parts, 1)
            if k:
                dve.wait_ge(b.z_parts, self.base + max(1, 2 * k - 2))
                v.tensor_tensor(b.z_lo[:, k - 1, :], b.z[:, k - 1, :], b.z_hi[:, k - 1, :],
                                ALU.subtract).then_inc(b.z_parts, 1)


class Rope(Stage):

    def __init__(self, b, m, needs):
        self.b, self.m, self.needs = b, m, needs
        self.swapped, self.turned = b.sem("rope_swapped"), b.sem("rope_turned")
        self.scaled, self.done_ = b.sem("rope_scaled"), b.sem("rope_done")
        self.done = (self.done_, 16)

    def tensor(self, pe):
        b, m = self.b, self.m
        for s, n in self.needs:
            pe.wait_ge(s, n)
        for i in range(16):
            if i >= 2:
                pe.wait_ge(self.turned, i - 1)
            for r, (t0, tn) in enumerate(RANGES2):
                ins = b.nc.tensor.matmul(b.ps[:, 2 * (i % 2) + r, 0:tn], m.swap, m.qk(i)[:, t0:t0 + tn],
                                         start=True, stop=True)
            ins.then_inc(self.swapped, 1)

    def gpsimd(self, pool):
        for i in range(16):
            pool.wait_ge(self.swapped, i + 1)
            x = self.m.qk(i)
            self.b.nc.gpsimd.tensor_tensor(x, x, self.m.cos, ALU.mult).then_inc(self.scaled, 1)

    def vector(self, dve):
        b, m, tt = self.b, self.m, self.b.nc.vector.tensor_tensor
        two = lambda ap: ap.rearrange("p (r t) -> p r t", r=2)
        for i in range(16):
            t = m.part[i % 2]
            dve.wait_ge(self.swapped, i + 1)
            if i >= 2:
                dve.wait_ge(self.done_, i - 1)
            tt(two(t), b.ps[:, 2 * (i % 2):2 * (i % 2) + 2, 0:L2 // 2], two(m.sin), ALU.mult).then_inc(self.turned, 1)
            dve.wait_ge(self.turned, i + 1)
            dve.wait_ge(self.scaled, i + 1)
            tt(m.qk(i), m.qk(i), t, ALU.add).then_inc(self.done_, 1)


class DiffAttention(Stage):

    def __init__(self, b, m, needs):
        self.b, self.m, self.needs = b, m, needs
        self.products = b.sem("da_products")
        self.summed = b.sem("da_summed")
        self.exped = b.sem("da_exped")
        self.scored = b.sem("da_scored")
        self.tail_scored = b.sem("da_tail_scored")
        self.maxed = b.sem("da_maxed")
        self.powered = b.sem("da_powered")
        self.probs = b.sem("da_probs")
        self.turned = b.sem("da_turned")
        self.kept = b.sem("da_kept")
        self.mixed = b.sem("da_mixed")
        self.out_main = b.sem("da_out_main")
        self.out_tail = b.sem("da_out_tail")
        self.nt = len(TOK_TILES)
        self.steps = DIFF_HEADS * self.nt
        self.done = [(self.out_tail, DIFF_HEADS)]

    def parts(self, n):
        h, tau = divmod(n, self.nt)
        t0, nt = TOK_TILES[tau]
        return h, tau, t0, nt, t0 + nt

    def tensor(self, pe):
        b, m, mm = self.b, self.m, self.b.nc.tensor.matmul
        for s, n in self.needs:
            pe.wait_ge(s, n)
        pe.wait_ge(self.products, 1)
        mm(b.ps[:, 6, 0:2], b.ones[0:DIFF_DIM, :], m.lam_prod[0:DIFF_DIM, :], start=True, stop=True).then_inc(self.summed, 1)
        for n in range(self.steps + 2):
            if n < self.steps:
                h, tau, t0, nt, nk = self.parts(n)
                if n >= 2:
                    pe.wait_ge(self.powered, 2 * n - 2)
                if tau == self.nt - 1 and h:
                    pe.wait_ge(self.out_tail, h)
                for c in range(2):
                    rows = slice(DIFF_DIM * c, DIFF_DIM * (c + 1))
                    q, k = m.qk(h)[rows, t0:t0 + nt], m.qk(8 + h)[rows]
                    ins = mm(b.ps[0:nt, 2 * (n % 2) + c, 0:min(nk, 512)], q, k[:, 0:min(nk, 512)], start=True, stop=True)
                    if nk > 512:
                        ins = mm(b.ps[0:nt, 7, 64 * c:64 * c + nk - 512], q, k[:, 512:nk], start=True, stop=True)
                        if c == 0:
                            ins.then_inc(self.tail_scored, 1)
                            pe.wait_ge(self.tail_scored, h + 1)
                ins.then_inc(self.scored, 1)
            if 1 <= n <= self.steps:
                j = n - 1
                h, tau, t0, nt, nk = self.parts(j)
                pe.wait_ge(self.probs, j + 1)
                if j >= 2:
                    pe.wait_ge(self.kept, j - 1)
                for i in range(tau + 1):
                    k0, kn = TOK_TILES[i]
                    ins = b.nc.tensor.transpose(b.ps[0:kn, 4 + j % 2, i * nt:(i + 1) * nt],
                                                m.prob[0:nt, j % 2, 0, k0:k0 + kn], b.ident[0:nt, 0:nt])
                ins.then_inc(self.turned, 1)
            if n >= 2:
                j = n - 2
                h, tau, t0, nt, nk = self.parts(j)
                pe.wait_ge(self.kept, j + 1)
                if tau == 0 and h:
                    pe.wait_ge(self.out_main, h)
                elif j == 0:
                    pe.wait_ge(self.exped, 1)
                o = b.ps[:, 6, t0:t0 + nt] if t0 < 512 else b.ps[:, 7, 128:128 + nt]
                for i in range(tau + 1):
                    kn = TOK_TILES[i][1]
                    ins = mm(o, m.v[0:kn, i, h * P:(h + 1) * P], m.prob_t[0:kn, j % 2, i * nt:(i + 1) * nt],
                             start=(i == 0), stop=(i == tau))
                ins.then_inc(self.mixed, 1)

    def scalar(self, act):
        b, m, f = self.b, self.m, self.b.nc.scalar.activation
        act.wait_ge(self.summed, 1)
        f(m.lam_exp, b.ps[:, 6, 0:2], ACT.Exp).then_inc(self.exped, 1)
        for n in range(self.steps + 3):
            if n < self.steps:
                h, tau, t0, nt, nk = self.parts(n)
                act.wait_ge(self.maxed, n + 1)
                if n >= 2:
                    act.wait_ge(self.turned, n - 1)
                for c in range(2):
                    main = min(nk, 512)
                    ins = f(m.prob[0:nt, n % 2, c, 0:main], b.ps[0:nt, 2 * (n % 2) + c, 0:main], ACT.Exp,
                            bias=m.negmax[0:nt, n % 2, c:c + 1], accum_out=m.total[0:nt, n % 2, c, 0:1])
                    if nk > 512:
                        ins = f(m.prob[0:nt, n % 2, c, 512:nk], b.ps[0:nt, 7, 64 * c:64 * c + nk - 512], ACT.Exp,
                                bias=m.negmax[0:nt, n % 2, c:c + 1], accum_out=m.total[0:nt, n % 2, c, 1:2])
                    ins.then_inc(self.powered, 1)
            if 1 <= n <= self.steps:
                j = n - 1
                h, tau, t0, nt, nk = self.parts(j)
                act.wait_ge(self.turned, j + 1)
                if j >= 2:
                    act.wait_ge(self.mixed, j - 1)
                if nt == P:
                    f(m.prob_t[:, j % 2, 0:(tau + 1) * nt], b.ps[:, 4 + j % 2, 0:(tau + 1) * nt], ACT.Copy).then_inc(self.kept, 1)
                else:
                    f(m.prob_t[:, j % 2, 0:tau * nt], b.ps[:, 4 + j % 2, 0:tau * nt], ACT.Copy)
                    kn = TOK_TILES[tau][1]
                    f(m.prob_t[0:kn, j % 2, tau * nt:(tau + 1) * nt], b.ps[0:kn, 4 + j % 2, tau * nt:(tau + 1) * nt],
                      ACT.Copy).then_inc(self.kept, 1)
            if n >= 3:
                j = n - 3
                h, tau, t0, nt, nk = self.parts(j)
                if tau == self.nt - 2:
                    act.wait_ge(self.mixed, j + 1)
                    f(m.o[:, h, 0:512], b.ps[:, 6, :], ACT.Copy).then_inc(self.out_main, 1)
                if tau == self.nt - 1:
                    act.wait_ge(self.mixed, j + 1)
                    f(m.o[:, h, 512:L2], b.ps[:, 7, 128:128 + nt], ACT.Copy).then_inc(self.out_tail, 1)

    def vector(self, dve):
        b, m, v = self.b, self.m, self.b.nc.vector
        tt, ts, stt = v.tensor_tensor, v.tensor_scalar, v.scalar_tensor_tensor
        for s, n in self.needs:
            dve.wait_ge(s, n)
        link = b.chain.link
        tt(m.lam_prod[0:DIFF_DIM, :], m.lam_in[0:DIFF_DIM, 0:4:2], m.lam_in[0:DIFF_DIM, 1:4:2], ALU.mult).then_inc(self.products, 1)
        dve.wait_ge(self.exped, 1)
        link(tt(m.lam, m.lam_exp[:, 1:2], m.lam_exp[:, 0:1], ALU.subtract))
        link(ts(m.lam, m.lam, -LAM_INIT, None, ALU.add))
        sub = b.cols[:, col_at("od_subln_w_2"):col_at("od_subln_w_2") + 1]
        link(ts(sub, sub, 1.0 - LAM_INIT, None, ALU.mult))
        for n in range(self.steps + 1):
            if n < self.steps:
                h, tau, t0, nt, nk = self.parts(n)
                dve.wait_ge(self.scored, n + 1)
                if n >= 2:
                    dve.wait_ge(self.powered, 2 * n - 2)
                hide = m.hide[0:nt, 0:nt].unsqueeze(1).broadcast_to([nt, 2, nt])
                if t0 < 512:
                    diag = b.ps[0:nt, 2 * (n % 2):2 * (n % 2) + 2, t0:t0 + nt]
                else:
                    diag = b.ps[0:nt, 7, 0:128].rearrange("p (c k) -> p c k", c=2)[:, :, 0:nt]
                link(tt(diag, diag, hide, ALU.add))
                main = min(nk, 512)
                ins = v.tensor_reduce(m.negmax[0:nt, n % 2, :], b.ps[0:nt, 2 * (n % 2):2 * (n % 2) + 2, 0:main], AX.X,
                                      ALU.max, negate=True)
                if nk > 512:
                    link(v.tensor_reduce(m.negmax2[0:nt, :], diag, AX.X, ALU.max, negate=True))
                    ins = tt(m.negmax[0:nt, n % 2, :], m.negmax[0:nt, n % 2, :], m.negmax2[0:nt, :], ALU.min)
                ins.then_inc(self.maxed, 1)
            if n >= 1:
                j = n - 1
                h, tau, t0, nt, nk = self.parts(j)
                dve.wait_ge(self.powered, 2 * j + 2)
                tot, inv = m.total[0:nt, j % 2, :, 0], m.inverse[0:nt, j % 2, :]
                if nk > 512:
                    link(tt(tot, tot, m.total[0:nt, j % 2, :, 1], ALU.add))
                link(v.reciprocal(inv, tot))
                tt(inv[:, 1:2], inv[:, 1:2], m.lam[0:nt], ALU.mult)
                p0, p1 = m.prob[0:nt, j % 2, 0, 0:nk], m.prob[0:nt, j % 2, 1, 0:nk]
                link(ts(p0, p0, inv[:, 0:1], None, ALU.mult))
                stt(out=p0, in0=p1, scalar=inv[:, 1:2], in1=p0, op0=ALU.mult, op1=ALU.add).then_inc(self.probs, 1)


COLS = {
    "norm_w": 16, "mem_norm_w": 8, "final_norm_w": 8, "gla_gate_bias": 4, "gla_out_norm_w": 4,
    "s5_d": 16, "s5_b_glu": 16, "norm_g_2": 64, "ev_mu_2": 14, "ev_w0_2": 4, "ev_a0_2": 4,
    "ev_k_k_2": 4, "ev_k_a_2": 4, "ev_r_k_2": 4, "ev_ln_w_2": 4, "ev_ln_b_2": 4,
    "ev_pool_scale_2": 4, "od_subln_w_2": 1,
}
EPSILONS = (1e-6, 1e-5, 64 * 1e-5)


def col_at(name):
    at = 0
    for n, w in COLS.items():
        if n == name:
            return at
        at += w
    raise KeyError(name)


def fm_units(w):
    k, m = w.shape
    u = w.reshape(k // 1024, 8, P, m // P, P).transpose(3, 0, 2, 1, 4)
    return u.reshape(-1, P, UNIT)


def tm_units(w):
    k, n = w.shape
    u = w.reshape(k // 256, 2, P, n // 512, 512).transpose(3, 0, 2, 1, 4)
    return u.reshape(-1, P, UNIT)


def weight_stream(i):
    g = i["gla_w_in"][0]
    kv = i["xa_w_kv"]
    parts = [fm_units(kv[0][:, :D]), tm_units(kv[0][:, D:]),
             fm_units(g[:, 3088 + MIX:]), fm_units(g[:, 3088:3088 + MIX]),
             fm_units(g[:, 0:512]), fm_units(g[:, 512:1024]), tm_units(g[:, 1024:3072]),
             fm_units(i["w_out"][0])]
    w = i["s5_w_in"][0]
    parts += [fm_units(w[:, :SEQ_W]), fm_units(kv[1][:, :D]), tm_units(kv[1][:, D:]),
              fm_units(w[:, SEQ_W + MIX:]), fm_units(w[:, 2 * SEQ_W:SEQ_W + MIX]), fm_units(w[:, SEQ_W:2 * SEQ_W]),
              fm_units(i["s5_w_glu"][0]), fm_units(i["w_out"][1])]
    od = i["od_w_in_2"][0]

    def mlp(layer):
        w1, w2 = i["mlp_w1_2"][layer], i["mlp_w2_2"][layer]
        n = w1.shape[1] // 2
        return [fm_units(w1[:, :n]), fm_units(w2[:n]), fm_units(w1[:, n:]), fm_units(w2[n:])]

    parts += [fm_units(i["ev_w_in_2"][0]), fm_units(i["ev_w_out_2"][0]),
              *mlp(0),
              fm_units(od[:, :D]), fm_units(od[:, D:2 * D]), tm_units(od[:, 2 * D:]),
              fm_units(i["od_w_out_2"][0]), *mlp(1)]
    return np.concatenate(parts, axis=0)


def s5_arrays(i):
    pg = lambda m: np.concatenate([m.T, m.T], axis=0)
    par = [np.concatenate([pg(m), m], axis=1) for m in (i["s5_lam_re"][0], i["s5_lam_im"][0])]
    step = i["s5_log_step"][0]
    par.append(np.concatenate([np.broadcast_to(step, (P, S5_G)), np.broadcast_to(step[:, None], (P, S5_P))], axis=1))
    twice = lambda m: np.concatenate([m, m], axis=0)
    blocks = lambda m: m.reshape(P, NB, 8 * S5_H).transpose(1, 0, 2)
    c = [blocks(twice(i[n][0].transpose(2, 0, 1))) for n in ("s5_c_re", "s5_c_im")]
    bp = [blocks(twice(i[n][0].transpose(1, 0, 2))) for n in ("s5_b_re", "s5_b_im")]
    bk = [i[n][0].transpose(2, 0, 1).reshape(S5_H, NB, 8 * S5_P).transpose(1, 0, 2) for n in ("s5_b_re", "s5_b_im")]
    return {"s5_par": np.stack(par, axis=1), "s5_c": np.stack(c, axis=2), "s5_ba": np.stack(bp, axis=2),
            "s5_bk": np.stack(bk, axis=2)}


def constants():
    t = np.arange(P)
    same = t[:, None] // CHUNK == t[None, :] // CHUNK
    restart = np.ones((P, L1), np.float32)
    restart[:, ::CHUNK] = 0
    return {
        "ident": np.eye(P, dtype=np.float32),
        "ones": np.ones((P, P), np.float32),
        "causal64": (same & (t[:, None] <= t[None, :])).astype(np.float32),
        "restart64": restart,
        "eps": np.tile(np.array(EPSILONS, np.float32), (P, 1)),
        "one": np.ones((P, 1), np.float32),
    }


def constants2():
    t = np.arange(P)
    row, col = t[:, None], t[None, :]
    chunk = row // RW_C == col // RW_C
    masks = [chunk & (col < row), chunk & (row < col), chunk & (row < col), chunk & (row <= col)]
    pair = row // RW_N == col // RW_N
    restart = np.ones((P, L2))
    restart[:, ::RW_C] = 0
    early = [2 ** (i + 1) / np.minimum(np.arange(16) + 1, 2 ** (i + 1)) for i in range(4)]
    c2 = np.concatenate([*masks, pair, pair, restart, np.tile(np.concatenate(early), (P, 1))], axis=1)
    inv = (np.float32(10000.0) ** (-np.arange(0, DIFF_DIM, 2, dtype=np.float32) / DIFF_DIM)).astype(np.float32)
    ang = (np.arange(L2, dtype=np.float32)[:, None] * inv[None, :]).astype(np.float32)
    cos, sin = (f(np.tile(ang, (1, 4))).T for f in (np.cos, np.sin))
    swap = np.zeros((P, P))
    for i in range(P):
        if i % DIFF_DIM < DIFF_DIM // 2:
            swap[i + DIFF_DIM // 2, i] = -1
        else:
            swap[i - DIFF_DIM // 2, i] = 1
    hide = np.where(col > row, -1e30, 0)
    c3 = np.concatenate([cos, sin, swap, hide], axis=1)
    return c2.astype(np.float32), c3.astype(np.float32)


class Views:
    pass


def build(nc, a, out):
    with ExitStack() as ctx:
        b = Board(nc, ctx)
        b.ps = ctx.enter_context(nc.psum_tensor("ps", [P, 8, 512], F32))
        b.x = b.sb("x", [P, KD, L2])
        b.h, b.h_r = b.sb_both("h", [P, KD, L2])
        b.ring, b.ring_r = b.sb_both("ring", [P, RING, UNIT])
        b.sq = b.sb("sq", [P, 2, 576])
        b.root = b.sb("root", [P, L2])
        b.inv = b.sb("inv", [P, L2])
        b.cols = b.sb("cols", [P, sum(COLS.values())])
        b.col = lambda name, k: b.cols[:, col_at(name) + k:col_at(name) + k + 1]
        tables = constants()
        held = {name: b.sb("c_" + name, list(t.shape)) for name, t in tables.items()}
        b.ident, b.ones, b.causal64, b.restart64 = (held[n] for n in ("ident", "ones", "causal64", "restart64"))
        b.eps = {e: held["eps"][:, i:i + 1] for i, e in enumerate(EPSILONS)}
        b.p = b.sb("p", [P, 2, N_MEM])
        b.negmax = b.sb("negmax", [P, 2])
        b.total = b.sb("total", [P, 4])
        b.memn = b.sb("memn", [P, KD, N_MEM])
        b.a8 = b.sb("a8", [P, 2, S5_G])
        with nc.sbuf_tensor("arena", [P, ARENA], F32) as arena:
            pass
        Z_TILES = MIX // P
        with ExitStack() as pieces:
            with nc.sbuf_tensor("z", [P, Z_TILES, L1], F32) as b.z:
                pass
            b.z_lo = pieces.enter_context(nc.sbuf_tensor("z_lo", [P, Z_TILES, L1], F32R))
            b.z_hi = pieces.enter_context(nc.sbuf_tensor("z_hi", [P, Z_TILES, L1], F32R))
        F_TILES = 16
        b.f, b.f_lo = b.sb_both("f", [P, F_TILES, L2])
        b.f_hi = b.sb("f_hi", [P, F_TILES, L2], F32R)
        PARTS_AT = 24576
        b.sb("below_parts", [P, PARTS_AT - 2 * F_TILES * L2])
        b.h_hi = b.sb("h_hi", [P, KD, L2], F32R)
        b.high = b.sb("high", [P, 2, UNIT], F32R)
        b.sb("above_parts", [P, ARENA - PARTS_AT - KD * L2 - 2 * UNIT])

        b.landed = [b.sem(f"landed{i}") for i in range(RING)]
        b.begun = b.sem("begun")
        b.filled = [b.sem("filled_even"), b.sem("filled_odd")]
        b.stored = [b.sem("stored_even"), b.sem("stored_odd")]
        b.squared, b.summed, b.rooted = b.sem("squared"), b.sem("summed"), b.sem("rooted")
        b.inverted, b.normed = b.sem("inverted"), b.sem("normed")
        b.norms = dict(squared=0, summed=0, rooted=0, inverted=0, ready=0, summed_onto=0, parts=0)
        b.out_hi, b.out_lo = b.sem("out_hi"), b.sem("out_lo")
        b.unit_hi, b.unit_lo = b.sem("unit_hi"), b.sem("unit_lo")
        b.z_parts = b.sem("z_parts")
        b.splits = 0
        b.summed_onto = b.sem("summed_onto")
        b.attentions = 0
        b.attention_sems = (
            b.sem("xa_scored"),
            b.sem("xa_maxed"),
            b.sem("xa_powered"),
            b.sem("xa_inverse"),
            b.sem("xa_scaled"),
            b.sem("xa_turned"),
            b.sem("xa_kept"),
            b.sem("xa_mixed"),
            b.sem("xa_gated"),
        )
        loaded = b.sem("loaded")
        written = b.sem("written")
        small = []
        small.append((b.x[:, :, :], a["x"]))
        small.append((b.cols[:, :], a["cols"]))
        for name in tables:
            small.append((held[name][:, :], a["c_" + name]))

        def view(off, *shape):
            n = int(np.prod(shape))
            ap = arena[:, off:off + n]
            if len(shape) == 1:
                return ap
            names = "abc"[:len(shape)]
            return ap.rearrange(f"p ({' '.join(names)}) -> p {' '.join(names)}",
                                **{c: s for c, s in zip(names[1:], shape[1:])})


        def copy(which, to, ps, scale=None):
            if which == "act":
                return nc.scalar.activation(to, ps, ACT.Copy, scale=1.0 if scale is None else scale)
            if scale is not None:
                return nc.vector.tensor_scalar(to, ps, scale, None, ALU.mult)
            return nc.vector.tensor_copy(to, ps)

        def keep(to, scale=None):
            return lambda which, m, parts, o: copy(which, to[:, m, :], parts[0], scale)

        BOTH, A, V = ("act", "dve"), ("act", "act"), ("dve", "dve")
        stages = []

        m0 = Views()
        m0.z = b.z
        m0.q = view(12288, 4, L1)
        m0.k = view(14336, 4, L1)
        m0.kend = view(24576, 4, L1)
        xq = view(12288, 8, L1)
        m0.v = view(16384, 4, SEQ_W)
        km = view(18432, KD, N_MEM)
        vm = view(20480, 2, D)
        b.pt = view(22528, 2, 2, L1)
        mem = view(16384, KD, N_MEM)
        h = b.h[:, :, :].rearrange("p k t -> p (k t)")
        m0.o = [h[:, i * 4 * L1:(i + 1) * 4 * L1].rearrange("p (e t) -> p e t", e=4) for i in range(2)]
        gt = view(26624, 7, L1)
        m0.t_a, m0.t_min, m0.t_neg, m0.t_cum, m0.e_pos, m0.e_neg, m0.e_end = (gt[:, i, :] for i in range(7))
        m0.t_exp, m0.t_log, m0.t_end = m0.t_neg, m0.e_neg, m0.t_neg
        m0.state = view(30208, 3, DV)
        m0.att = view(31744, 2, P)
        m0.ktok = view(32000, 2, P)
        m0.decay = view(33408, GLA_HEADS, 8)
        m0.rank = view(32256, L1)
        m0.w_rank = view(32768, KD, RANK)
        m0.w_up = view(32896, 512)
        small.append((mem, a["mem"]))
        small.append((m0.w_rank[:, :, :], a["w_rank"]))
        small.append((m0.w_up[0:RANK, :], a["w_up"]))
        loads_in = (loaded, 16 * len(small))

        rms = Rms(b, lambda k: mem[:, k, :], KD, MEMS, D, EPS, lambda k: b.col("mem_norm_w", k),
                  lambda k: b.memn[:, k, :], [0], [loads_in], [loads_in])
        stages.append(rms)
        mem_ready = rms.ready
        x1 = lambda k: b.x[:, k, META:]
        rms = Rms(b, x1, KD, FULL, D, EPS, lambda k: b.col("norm_w", k),
                  lambda k: b.h[:, k, 0:L1], [1], [])
        stages.append(rms)
        h1 = lambda k: b.h[:, k, 0:L1]
        memn = lambda k: b.memn[:, k, :]
        MEM_TILES = [(0, P), (P, P)]
        TILES1 = [(t * P, P) for t in range(4)]

        def tm_keep(to, width=512):
            return lambda which, m, part, o: copy(
                which, to[0:part.shape[0], m[1], bass.ds(m[0] * width, width)], part)

        b.d_q = nc.dram_tensor("d_q", [2, S5_C, S5_G * S5_P], F32).ap()
        b.d_ca = nc.dram_tensor("d_ca", [NB, P, 8, 160], F32).ap()
        b.d_pb = nc.dram_tensor("d_pb", [NB, P, 8, P], F32).ap()
        b.d_k = nc.dram_tensor("d_k", [NB, S5_H, 8, 240], F32).ap()
        b.d_u = nc.dram_tensor("d_u", [SEQ_W, L1], F32).ap()
        b.d_y = nc.dram_tensor("d_y", [SEQ_W, L1], F32).ap()
        t5 = Views()
        t5.e = view(22528, 2, 9, S5_G)
        t5.f = view(24832, 2, S5_G)
        t5.ca = [view(25088 + 1280 * i, 8, 160) for i in range(2)]
        t5.pb = [view(27648 + 1024 * i, 8, P) for i in range(2)]
        t5.qk = [view(29696 + 1024 * i, 2, 512) for i in range(2)]
        t5.bk = [view(31744, 2, 512), view(16384, 2, 512)]
        t5.cin = [view(17408 + 256 * i, 2, P) for i in range(2)]
        t5.bin = [view(17920 + 256 * i, 2, P) for i in range(2)]
        t5.tmp = b.sq[:, :, :].rearrange("p a t -> p (a t)")
        t5.q = view(25088, 2, S5_C, S5_P)
        t5.pow = view(26112, 2, 9, 192)
        t5.par = view(29696, 13, 192)
        tables = S5Tables(b, t5, a, [rms.ready, (b.summed, 2 * KD)])
        stages.append(tables)
        stages.append(Gemm(b, "mem_k", "fm", memn, KD, KD, MEMS, keep(km), A, [mem_ready, rms.rooted]))
        stages.append(Gemm(b, "mem_v", "tm", memn, KD, 2, None, tm_keep(vm), A, [], MEM_TILES))
        stages.append(Gemm(b, "xq", "fm", h1, KD, KD, FULL, keep(xq, 1 / 16), A, [rms.ready]))
        stages.append(Gemm(b, "z", "fm", h1, KD, MIX // P, FULL,
                           lambda which, m, parts, o: nc.scalar.activation(m0.z[:, m, :], parts[0], ACT.Silu), A, []))
        g = stages[-1]
        h_hi = lambda k: b.h_hi[:, k, :]
        h1_lo = lambda k: b.h_r[:, k, 0:L1]
        h_split = b.sem("h_split")
        split_needs = [(b.stored[0], g.done[0]), (b.stored[1], g.done[1])] + tables.done

        class SplitH(Stage):

            def vector(self, dve):
                for s, n in split_needs:
                    dve.wait_ge(s, n)
                for k in range(KD):
                    copied = nc.vector.tensor_copy(h_hi(k)[:, 0:L1], h1(k))
                b.chain.link(copied)
                for k in range(KD):
                    nc.vector.tensor_tensor(h1_lo(k), h1(k), h_hi(k)[:, 0:L1], ALU.subtract).then_inc(h_split, 1)
        stages.append(SplitH())
        att = MemoryAttention(b, "xa0", lambda k: xq[:, k, :], lambda k: km[:, k, :], vm,
                              lambda k: m0.z[:, 16 + k, :],
                              [(b.stored[0], g.done[0]), (b.stored[1], g.done[1])] + tables.done)
        stages.append(att)
        parts1 = dict(high=b.high, x_hi=h_hi)
        stages.append(Gemm(b, "q", "fm", h1_lo, KD, 4, FULL, keep(m0.q), BOTH, [att.done, (h_split, KD)], **parts1))
        stages.append(Gemm(b, "k", "fm", h1_lo, KD, 4, FULL, keep(m0.k), BOTH, [], **parts1))
        stages.append(Gemm(b, "v", "tm", h1_lo, KD, 4, None, tm_keep(m0.v), BOTH, [], TILES1, **parts1))
        g = stages[-1]
        gla = Gla(b, m0, [(b.stored[0], g.done[0]), (b.stored[1], g.done[1])])
        stages.append(gla)

        def add_x(which, m, parts, o):
            return nc.vector.tensor_tensor(b.x[:, m, META:], b.x[:, m, META:], parts[0], ALU.add)
        z_lo, z_hi = (lambda k: b.z_lo[:, k, :]), (lambda k: b.z_hi[:, k, :])
        split_z = SplitZ(b, 0, [gla.done])
        stages.append(split_z)
        stages.append(Gemm(b, "out0", "fm", z_lo, Z_TILES, KD, FULL, add_x, V, [gla.done], high=b.high, x_hi=z_hi,
                           ready=split_z.ready))
        g = stages[-1]

        m5 = Views()
        high = b.high
        out0_done = [(b.stored[0], g.done[0]), (b.stored[1], g.done[1])]
        perm = lambda ap: ap.rearrange("p (j k) -> p k j", k=S5_C)
        chunked = lambda ap: ap.rearrange("p (k j) -> p k j", k=S5_C)
        h1_lo = lambda k: b.h_r[:, k, 0:L1]
        rms = Rms(b, x1, KD, FULL, D, EPS, lambda k: b.col("norm_w", 8 + k),
                  lambda k: chunked(b.h[:, k, 0:L1]), [0], [], out0_done, view=perm, each=g.tile,
                  hi=lambda k: chunked(h_hi(k)[:, 0:L1]), lo=lambda k: chunked(h1_lo(k)))
        stages.append(rms)
        u_stage = [view(12288 + 512 * i, L1) for i in range(4)]
        u_sent = [b.sem(f"u_sent{i}") for i in range(4)]

        def send_u(act, m, o, par, n):
            act.wait_ge(b.stored[par], n)
            act.dma_start(b.d_u.rearrange("(m p) t -> m p t", p=P)[m], u_stage[o]).then_inc(u_sent[o], 16)

        stages.append(Gemm(b, "u", "fm", h1_lo, KD, NB, FULL,
                           lambda which, m, parts, o: copy(which, u_stage[o], parts[0]), A, [rms.ready],
                           before=lambda eng, o, it: eng.wait_ge(u_sent[o], it * 16),
                           high=high, x_hi=h_hi, after=send_u))
        rms.feed(stages[-1])
        u_all = [(u_sent[o], 16 * NB // 4) for o in range(4)]
        km1, vm1, xq1 = view(14336, KD, N_MEM), view(12288, 2, D), view(18432, 8, L1)
        stages.append(Gemm(b, "mem_k1", "fm", memn, KD, KD, MEMS, keep(km1), BOTH, []))
        stages.append(Gemm(b, "mem_v1", "tm", memn, KD, 2, None, tm_keep(vm1), BOTH, u_all, MEM_TILES))
        stages.append(Gemm(b, "xq1", "fm", h1_lo, KD, KD, FULL, keep(xq1, 1 / 16), BOTH, [], high=high, x_hi=h_hi))
        stages.append(Gemm(b, "z1_xa", "fm", h1_lo, KD, D // P, FULL,
                           lambda which, m, parts, o: nc.scalar.activation(m0.z[:, m + 16, :], parts[0], ACT.Silu), A, [],
                           high=high, x_hi=h_hi))
        g = stages[-1]
        xa_done = [(b.stored[0], g.done[0]), (b.stored[1], g.done[1])]
        rejoined = b.sem("rejoined")

        class Rejoin(Stage):

            def vector(self, dve):
                for s, n in xa_done:
                    dve.wait_ge(s, n)
                for k in range(KD):
                    nc.vector.tensor_tensor(b.h[:, k, 0:L1], h1_lo(k), h_hi(k)[:, 0:L1], ALU.add).then_inc(rejoined, 1)
        stages.append(Rejoin())
        att = MemoryAttention(b, "xa1", lambda k: xq1[:, k, :], lambda k: km1[:, k, :], vm1,
                              lambda k: m0.z[:, 16 + k, :],
                              [(b.stored[0], g.done[0]), (b.stored[1], g.done[1])])
        stages.append(att)
        m5.u = view(25408, S5_G, S5_J)
        m5.y = view(25408, NB, L1)
        m5.state = view(12288, S5_J + 1, S5_G)
        m5.ca = [view(20608, 8, 160), view(21888, 8, 160)]
        m5.pb = [view(23168, 8, P), view(24192, 8, P)]
        m5.toep = m5.pb
        hf = b.h[:, :, :].rearrange("p k t -> p (k t)")
        memf = b.memn[:, :, :].rearrange("p k t -> p (k t)")
        m5.kpad = [memf[32 * i:32 * i + S5_H, 0:1920].rearrange("p (g n) -> p g n", g=8) for i in range(2)]
        m5.t1, m5.t2 = b.p[:, 0, 0:P], b.p[:, 1, 0:P]
        m5.ystage = [hf[:, i * 512:(i + 1) * 512].rearrange("p (g j) -> p g j", g=8) for i in range(2)]
        m5.ustage = [hf[:, i * 512:(i + 1) * 512] for i in (2, 3)]
        s5i = S5Inputs(b, m5, u_all + [(rejoined, KD)], [att.done])
        stages.append(s5i)
        gz = Gemm(b, "z1", "fm", h1, KD, NB, FULL,
                  lambda which, m, parts, o: nc.scalar.activation(m0.z[:, m, :], parts[0], ACT.Silu), A,
                  [(s5i.x_kept, NB), (s5i.k_kept, NB), (rejoined, KD)])
        stages.append(gz)
        stages.append(S5Scan(b, m5, [s5i.done]))
        s5o = S5Outputs(b, m5, [(b.stored[0], gz.done[0]), (b.stored[1], gz.done[1]), stages[-1].done, (s5i.added, NB), (s5i.k_stored[0], 8 * NB), (s5i.k_stored[1], 8 * NB)])
        stages.append(s5o)
        gate = [hf[:, i * 512:(i + 1) * 512] for i in range(4)]
        glu_gated = b.sem("glu_gated")
        glu = Gemm(b, "glu", "fm", lambda k: m5.y[:, k, :], 16, NB, FULL,
                   lambda which, m, parts, o: nc.scalar.activation(
                       gate[o], parts[0], ACT.Sigmoid,
                       bias=b.cols[:, bass.ds(m + col_at("s5_b_glu"), 1)]), A, [s5o.done],
                   before=lambda eng, o, it: eng.wait_ge(glu_gated, it * 8 + 2 * o - 6))
        stages.append(glu)

        class GluGate(Stage):

            def vector(self, dve):
                with dve.Fori(0, NB // 4) as it:
                    for o in range(4):
                        par, n = glu.count(o, it)
                        dve.wait_ge(b.stored[par], n)
                        nc.vector.tensor_tensor(gate[o], gate[o], m5.y[:, it * 4 + o, :], ALU.mult).then_inc(glu_gated, 1)
                        dve.wait_ge(glu_gated, it * 8 + 2 * o + 1)
                        z = m0.z[:, it * 4 + o, :]
                        nc.vector.tensor_tensor(z, z, gate[o], ALU.mult).then_inc(glu_gated, 1)
        stages.append(GluGate())

        def add_x1(which, m, parts, o):
            x = perm(b.x[:, m, META:])
            return nc.vector.tensor_tensor(x, x, parts[0].rearrange("p (k j) -> p k j", k=S5_C), ALU.add)
        split_z = SplitZ(b, 1, [(glu_gated, 2 * NB)])
        stages.append(split_z)
        stages.append(Gemm(b, "out1", "fm", z_lo, Z_TILES, KD, FULL, add_x1, V, [(glu_gated, 2 * NB)], high=high,
                           x_hi=z_hi, ready=split_z.ready))
        g = stages[-1]

        done = lambda g: [(b.stored[0], g.done[0]), (b.stored[1], g.done[1])]
        rms = Rms(b, x1, KD, FULL, D, EPS, lambda k: b.col("final_norm_w", k), x1, [0], [], done(g), each=g.tile)
        stages.append(rms)

        memf = b.memn[:, :, :].rearrange("p k t -> p (k t)")
        b.masks = memf[:, 0:4 * P].rearrange("p (i s) -> p i s", i=4)
        b.same64, b.ones64 = memf[:, 4 * P:5 * P], memf[:, 5 * P:6 * P]
        b.restart32, b.early = memf[:, 6 * P:6 * P + L2], memf[:, 6 * P + L2:6 * P + L2 + 64]
        c2 = memf[:, 0:6 * P + L2 + 64]
        m2 = Views()
        y2 = view(0, 18, L2)
        m2.y = lambda i: y2[:, i, :]
        m2.y4 = y2[:, 0:4, :]
        al, be, gg, bv = (view(9504 + 2112 * i, 4, L2) for i in range(4))
        m2.al, m2.be, m2.g, m2.bonus = (lambda j, t=t: t[:, j, :] for t in (al, be, gg, bv))
        m2.o4 = view(17952, 4, L2)
        (m2.t_w, m2.t_cum, m2.t_pos, m2.t_neg, m2.t_before, m2.t_norm, m2.t_a, m2.t_k, m2.t_bonus,
         m2.t_sq) = (view(20064 + L2 * i, L2) for i in range(10))
        m2.end = view(32096 + 1280, 4, 17)
        m2.rest_a, m2.one, m2.one2 = view(33444, 4), view(33448, 1), view(33449, 1)
        o_ = [20064]

        def take(*shape):
            ap = view(o_[0], *shape)
            o_[0] += int(np.prod(shape))
            return ap
        m2.p = take(8, RW_N).rearrange("p (s q) k -> p s q k", s=2)
        m2.gram = take(4, 4 * P).rearrange("p q (i s) -> p q i s", i=4)
        m2.mk, m2.inv, m2.au = take(4, P), take(4, P), take(4, P)
        m2.pw = take(4, 4 * P).rearrange("p (l z) (q s) -> p l z q s", l=2, q=4)
        m2.bkv = take(6, P).rearrange("p (a i) k -> p a i k", a=2)
        m2.a = take(16, P).rearrange("p (j c) k -> p j c k", j=4)
        m2.bb = take(16, P).rearrange("p (j c) k -> p j c k", j=4)
        m2.s = take(8, P).rearrange("p (l j) k -> p l j k", l=2)
        assert o_[0] <= 32096
        m2.w_wa, m2.w_g = view(32096, 512), view(32608, 512)
        m2.w_pool = b.p[:, :, :].rearrange("p a (i k) -> p (a i) k", i=2)
        m2.sums = [b.h[:, 0, :], b.h[:, 1, :]]
        second = b.sem("tables_loaded")
        second_in = (second, 16 * 6)

        out1_done = done(g)

        class LoadSecond(Stage):

            def gpsimd(self, pool):
                for s, n in out1_done:
                    pool.wait_ge(s, n)
                for to, fro in ((c2, a["c2"]), (m2.w_wa[0:64], a["w_decay"]), (m2.w_wa[64:P], a["w_rate"]),
                                (m2.w_g, a["w_gate"]), (m2.w_pool, a["w_pool"]), (m2.one2, a["c_one"])):
                    pool.dma_start(to, fro).then_inc(second, 16)
        stages.append(LoadSecond())
        x2 = lambda k: b.x[:, k, :]
        h2 = lambda k: b.h[:, k, :]

        def norm_g(layer, i):
            return lambda k: b.col("norm_g_2", (4 * layer + i) * 8 + k)

        def keep2(to, scale=None):
            def store(which, m, parts, o):
                ps = b.ps[:, 2 * (o % 2):2 * (o % 2) + 2, 0:L2 // 2]
                return copy(which, to(m).rearrange("p (r t) -> p r t", r=2), ps, scale)
            return store

        def post(layer, i, g):
            rms = Rms(b, h2, KD, HALVES, D, EPS, norm_g(layer, i), h2, [0, 1], [], done(g), onto=x2, each=g.tile)
            stages.append(rms)
            return rms

        h2_lo = lambda k: b.h_r[:, k, :]

        def pre(layer, i, before):
            rms = Rms(b, x2, KD, HALVES, D, EPS, norm_g(layer, i), h2, [2, 3], [], hi=h_hi, lo=h2_lo, each=before.tile)
            stages.append(rms)
            return rms

        def gemm(name, x, kt, outs, store, engines, needs, high=None, x_hi=None):
            g = Gemm(b, name, "fm", x, kt, outs, HALVES, store, engines, needs, high=high, x_hi=x_hi)
            stages.append(g)
            return g

        rms = pre(0, 0, rms)
        ga = gemm("ev_a", h2_lo, KD, 12, keep2(lambda m: y2[:, m, :]), A, [rms.ready], high, h_hi)
        rms.feed(ga)
        gb = gemm("ev_b", h2_lo, KD, 6, keep2(lambda m: y2[:, 12 + m, :]), A, [], high, h_hi)
        shift = Shift(b, lambda m: y2[:, m, :], m2.t_w,
                      [(m, (b.stored[m % 2], ga.full0[m % 2] + m // 2 + 1)) for m in range(14)])
        shift.tiles = [t if t[0] < 12 else (t[0], (b.stored[t[0] % 2], gb.full0[t[0] % 2] + (t[0] - 12) // 2 + 1))
                       for t in shift.tiles]
        stages.append(shift)
        prep = RwkvPrepare(b, m2, [(shift.shifted, 14), second_in] + done(gb))
        stages.append(prep)
        pool_ = Pool(b, m2, [second_in] + done(gb))
        rw = Rwkv(b, m2, [prep.done], pool_)
        stages.append(rw)
        fin = RwkvFinish(b, m2, rw.done, pool_)
        stages.append(fin)
        mixed = lambda k: m2.o4[:, k, :] if k < 4 else y2[:, 10 + k, :]
        g1 = gemm("ev_out", mixed, KD, KD, keep2(lambda m: b.h[:, m, :]), BOTH, [fin.done, pool_.done])
        rms = post(0, 1, g1)

        mlp_parts = b.sem("mlp_parts")

        def mlp(layer, rms):
            f, f_lo, f_hi = b.f, b.f_lo, b.f_hi
            first = view(2 * F_TILES * L2, KD, L2)
            rms = pre(layer, 2, rms)

            def relu(which, m, parts, o):
                to = f[:, m, :].rearrange("p (r t) -> p r t", r=2)
                return nc.scalar.activation(to, b.ps[:, 2 * (o % 2):2 * (o % 2) + 2, 0:L2 // 2], ACT.Relu)

            def both_halves(which, m, parts, o):
                two = lambda ap: ap.rearrange("p (r t) -> p r t", r=2)
                return nc.vector.tensor_tensor(two(b.h[:, m, :]), two(first[:, m, :]),
                                               b.ps[:, 2 * (o % 2):2 * (o % 2) + 2, 0:L2 // 2], ALU.add)

            class Squares(Stage):

                def __init__(self, g, base):
                    self.g, self.base = g, base

                def vector(self, dve):
                    with dve.Fori(0, 4) as it:
                        for o in range(4):
                            par, n = self.g.count(o, it)
                            done = it * 12 + (self.base + 3 * o)
                            dve.wait_ge(b.stored[par], n)
                            t, hi, lo = f[:, it * 4 + o, :], f_hi[:, it * 4 + o, :], f_lo[:, it * 4 + o, :]
                            nc.vector.tensor_tensor(t, t, t, ALU.mult).then_inc(mlp_parts, 1)
                            dve.wait_ge(mlp_parts, done + 1)
                            nc.vector.tensor_copy(hi, t).then_inc(mlp_parts, 1)
                            dve.wait_ge(mlp_parts, done + 2)
                            nc.vector.tensor_tensor(lo, t, hi, ALU.subtract).then_inc(mlp_parts, 1)

            for half in range(2):
                base = 48 * (2 * layer + half)
                g = gemm(f"mlp{layer}_in{half}", h2_lo, KD, 16, relu, A, [rms.ready], high, h_hi)
                if half == 0:
                    rms.feed(g)
                stages.append(Squares(g, base))
                store, engines = (both_halves, V) if half else (keep2(lambda m: first[:, m, :]), BOTH)
                g2 = gemm(f"mlp{layer}_out{half}", lambda k: f_lo[:, k, :], 16, KD, store, engines,
                          [(mlp_parts, base + 48)], high, lambda k: f_hi[:, k, :])
            return post(layer, 3, g2)

        rms = mlp(0, rms)

        rms = pre(1, 0, rms)
        m3 = Views()
        qk = view(0, 16, L2)
        m3.qk = lambda i: qk[:, i, :]
        m3.v = view(8448, 5, D)
        m3.o = view(13568, 8, L2)
        m3.prob = view(17792, 4, L2).rearrange("p (l c) t -> p l c t", l=2)
        m3.prob_t = view(19904, 2, 512)
        m3.cos, m3.sin, m3.swap, m3.hide = view(20928, L2), view(21456, L2), view(21984, P), view(22112, P)
        m3.lam_in = view(22240, 4)
        m3.part = [view(22244 + L2 * i, L2) for i in range(2)]
        tiny = lambda off, n: view(23300 + off, n)
        m3.negmax = view(23300, 2, 2)
        m3.total = tiny(4, 8).rearrange("p (l c i) -> p l c i", l=2, c=2)
        m3.inverse, m3.negmax2 = view(23312, 2, 2), tiny(16, 2)
        m3.lam_prod, m3.lam_exp, m3.lam = tiny(18, 2), tiny(20, 2), tiny(22, 1)
        third = second
        before3 = rms.at["ready"]

        class LoadThird(Stage):

            def gpsimd(self, pool):
                pool.wait_ge(b.normed, before3)
                pool.dma_start(view(20928, 1312), a["c3"]).then_inc(third, 16)
                pool.dma_start(m3.lam_in[0:DIFF_DIM], a["lam"]).then_inc(third, 16)
        stages.append(LoadThird())
        third_in = (third, second_in[1] + 32)
        gq = gemm("od_q", h2_lo, KD, KD, keep2(lambda m: qk[:, m, :], 0.125), BOTH, [rms.ready], high, h_hi)
        rms.feed(gq)
        gk = gemm("od_k", h2_lo, KD, KD, keep2(lambda m: qk[:, m + 8, :]), BOTH, [], high, h_hi)
        gv = Gemm(b, "od_v", "tm", h2_lo, KD, 2, None, tm_keep(m3.v), BOTH, [], TOK_TILES, high=high, x_hi=h_hi)
        stages.append(gv)
        rope = Rope(b, m3, done(gv) + [third_in])
        stages.append(rope)
        da = DiffAttention(b, m3, [rope.done, third_in])
        stages.append(da)
        subs = []
        for h in range(8):
            o = lambda k, h=h: m3.o[:, h, :]
            subs.append(Rms(b, o, 1, HALVES, P, 1e-5, lambda k: b.col("od_subln_w_2", 0), o,
                            [2 * (h % 2), 2 * (h % 2) + 1], da.done, [subs[-1].rooted] if h else da.done))
            stages.append(subs[-1])
        g1 = gemm("od_out", lambda k: m3.o[:, k, :], KD, KD, keep2(lambda m: b.h[:, m, :]), BOTH, [subs[-1].ready])
        rms = post(1, 1, g1)
        rms = mlp(1, rms)

        block = ctx.enter_context(nc.Block())
        n_units = b.units

        @block.sync
        def _(sp):
            def load(u, slot):
                sp.dma_start(b.ring[:, slot, :], a["units"][u]).then_inc(b.landed[slot], 16)
            for u in range(RING):
                load(u, u)
            rounds = n_units // RING
            with sp.Fori(1, rounds) as r:
                for j in range(RING):
                    sp.wait_ge(b.begun, r * RING + j - RING + 2)
                    load(r * RING + j, j)
            for u in range(rounds * RING, n_units):
                sp.wait_ge(b.begun, u - RING + 2)
                load(u, u % RING)
            for k in range(KD):
                sp.wait_ge(*rms.tile(k))
                sp.dma_start(out[:, k, :], b.x[:, k, META:]).then_inc(written, 16)
            sp.wait_ge(written, 16 * KD)

        @block.gpsimd
        def _(pool):
            for stage in stages:
                stage.gpsimd(pool)

        @block.tensor
        def _(pe):
            pe.wait_ge(*loads_in)
            for stage in stages:
                stage.tensor(pe)

        @block.scalar
        def _(act):
            for to, fro in small:
                act.dma_start(to, fro).then_inc(loaded, 16)
            for stage in stages:
                stage.scalar(act)

        @block.vector
        def _(dve):
            b.chain = Chain(dve, b.sem("vector_steps"))
            dve.wait_ge(*loads_in)
            for stage in stages:
                stage.vector(dve)


def kernel(**inputs):
    import concourse.bacc as _bacc
    from concourse.bass_utils import run_bass_kernel_spmd as _run

    i = {k: np.ascontiguousarray(v) for k, v in inputs.items()}
    tiles = lambda m: np.ascontiguousarray(m.T.reshape(m.shape[1] // P, P, m.shape[0]).transpose(1, 0, 2))
    arrays = {
        "units": weight_stream(i),
        "x": tiles(i["x"][0]),
        "mem": tiles(i["mem"][0]),
        "cols": np.concatenate([i[n].reshape(-1, P).T for n in COLS], axis=1),
        "w_rank": i["gla_w_in"][0][:, 3072:3088].reshape(KD, P, RANK).transpose(1, 0, 2),
        "w_up": i["gla_w_gate_up"][0],
    }
    arrays.update(s5_arrays(i))
    arrays["c2"], arrays["c3"] = constants2()
    arrays.update({
        "x": np.concatenate([tiles(i["meta_2"]), tiles(i["x"][0])], axis=2),
        "w_decay": i["ev_w_up_2"][0], "w_rate": i["ev_a_up_2"][0], "w_gate": i["ev_g_up_2"][0],
        "w_pool": i["ev_pool_w_2"][0].transpose(1, 0, 2),
        "lam": i["od_lambda_2"][0].T,
    })
    arrays.update({"c_" + n: t for n, t in constants().items()})
    arrays = {n: np.ascontiguousarray(v) for n, v in arrays.items()}
    nc = _bacc.Bacc("TRN2", target_bir_lowering=False, num_devices=1)
    a = {n: nc.dram_tensor("in_" + n, v.shape, F32, kind="ExternalInput").ap() for n, v in arrays.items()}
    out = nc.dram_tensor("out", (P, KD, L1), F32, kind="ExternalOutput").ap()
    build(nc, a, out)
    r = _run(nc, [{"in_" + n: v for n, v in arrays.items()}], core_ids=[0])
    return np.ascontiguousarray(r.results[0]["out"].transpose(2, 1, 0).reshape(1, L1, D))
```
